# Optimizing a Trainium2 kernel written in Bass

```python
import jax, jax.numpy as jnp
from jax import lax
import numpy as np

D_MODEL = 1024
BATCH = 1
SEQ = 512
DEPTH = 2

GRID_W = 64
CTX_LEN = 256
HEAD_DIM = 64
GROUP_W = D_MODEL // 4
A_HEADS = GROUP_W // HEAD_DIM
A_KV = A_HEADS // 2
B_HEADS = GROUP_W // HEAD_DIM
B_KV = B_HEADS // 2
F_CH = 64
F_GROUPS = GROUP_W // F_CH
R_HEADS = GROUP_W // HEAD_DIM
MIX_W = 4 * GROUP_W
Q_BLOCK = 128
WINDOW = 128
RET_CHUNK = 128
ROPE_THETA = 10000.0
FF_DIM = -(-8 * D_MODEL // (3 * 256)) * 256
ALPHA = (2.0 * DEPTH) ** 0.25
BETA = (8.0 * DEPTH) ** -0.25
NORM_EPS = 1e-6
NEG_INF = -1e30
F32 = jnp.float32
SPLITS = (A_HEADS * HEAD_DIM, A_KV * HEAD_DIM, A_KV * HEAD_DIM,
          B_HEADS * HEAD_DIM, B_KV * HEAD_DIM, B_KV * HEAD_DIM,
          F_GROUPS * F_CH,
          GROUP_W, GROUP_W, GROUP_W, GROUP_W)
SPLIT_IDX = tuple(int(i) for i in np.cumsum(SPLITS)[:-1])
IN_W = sum(SPLITS)

kernel_name = 'hybrid_parallel_group_dit_block'

def layer_norm(x, w=None, b=None):
    xf = x.astype(F32)
    mu = jnp.mean(xf, -1, keepdims=True)
    var = jnp.mean(jnp.square(xf - mu), -1, keepdims=True)
    y = (xf - mu) * lax.rsqrt(var + NORM_EPS)
    if w is not None:
        y = y * w.astype(F32) + b.astype(F32)
    return y.astype(x.dtype)

def rms_norm(x, w):
    xf = x.astype(F32)
    y = xf * lax.rsqrt(jnp.mean(jnp.square(xf), -1, keepdims=True) + NORM_EPS) * w.astype(F32)
    return y.astype(x.dtype)

def modulate(x, shift, scale):
    return layer_norm(x) * (1.0 + scale) + shift

def post_norm(x, y, w, b):
    return layer_norm(ALPHA * x + y, w, b)

def heads(t):
    return t.reshape(t.shape[:-1] + (t.shape[-1] // HEAD_DIM, HEAD_DIM))

def group_q(q, n_kv):
    return q.reshape(q.shape[:2] + (n_kv, q.shape[2] // n_kv, q.shape[3]))

def rope_tables(pos, n_freq):
    inv = ROPE_THETA ** (-jnp.arange(n_freq, dtype=F32) / n_freq)
    ang = pos[:, None] * inv[None, :]
    return jnp.cos(ang), jnp.sin(ang)

def rotate(x, cos, sin):
    f = cos.shape[-1]
    c = cos[None, :, None, :].astype(x.dtype)
    s = sin[None, :, None, :].astype(x.dtype)
    x1, x2 = x[..., :f], x[..., f:]
    return jnp.concatenate([x1 * c - x2 * s, x2 * c + x1 * s], -1)

def rope_2d(x, tab):
    cos_r, sin_r, cos_c, sin_c = tab
    h = x.shape[-1] // 2
    return jnp.concatenate([rotate(x[..., :h], cos_r, sin_r), rotate(x[..., h:], cos_c, sin_c)], -1)

def gqa_attend(q, k, v, sink):
    s = jnp.einsum('bqkgd,bskd->bkgqs', q, k).astype(F32) * (q.shape[-1] ** -0.5)
    if sink is not None:
        snk = jnp.broadcast_to(sink.astype(F32)[None, :, :, None, None], s.shape[:-1] + (1,))
        p = jax.nn.softmax(jnp.concatenate([s, snk], -1), axis=-1)[..., :-1]
    else:
        p = jax.nn.softmax(s, axis=-1)
    o = jnp.einsum('bkgqs,bskd->bqkgd', p.astype(v.dtype), v)
    return o.reshape(o.shape[:2] + (-1,))

def global_attention(q, k, v):
    B, S, KV, G, d = q.shape
    nb = S // Q_BLOCK
    qb = jnp.moveaxis(q.reshape(B, nb, Q_BLOCK, KV, G, d), 1, 0)
    o = lax.map(lambda blk: gqa_attend(blk, k, v, None), qb)
    return jnp.moveaxis(o, 0, 1).reshape(B, S, -1)

def window_attention(q, k, v, k_c, v_c, sink):
    B, S, KV, G, d = q.shape
    nb = S // Q_BLOCK
    w3 = 3 * Q_BLOCK
    lc = k_c.shape[1]
    qb = q.reshape(B, nb, Q_BLOCK, KV, G, d)

    def band(t):
        tp = jnp.pad(t, ((0, 0), (Q_BLOCK, Q_BLOCK), (0, 0), (0, 0))).reshape(B, nb + 2, Q_BLOCK, KV, d)
        return jnp.concatenate([tp[:, :-2], tp[:, 1:-1], tp[:, 2:]], axis=2)

    kw, vw = band(k), band(v)
    scale = d ** -0.5
    s_loc = jnp.einsum('bnqkgd,bnskd->bnkgqs', qb, kw).astype(F32) * scale
    blk = jnp.arange(nb, dtype=jnp.int32)[:, None]
    qpos = blk * Q_BLOCK + jnp.arange(Q_BLOCK, dtype=jnp.int32)[None, :]
    kpos = (blk - 1) * Q_BLOCK + jnp.arange(w3, dtype=jnp.int32)[None, :]
    kp = kpos[:, None, :]
    valid = (jnp.abs(kp - qpos[:, :, None]) <= WINDOW) & (kp >= 0) & (kp < S)
    s_loc = jnp.where(valid[None, :, None, None], s_loc, NEG_INF)
    s_ctx = jnp.einsum('bnqkgd,bskd->bnkgqs', qb, k_c).astype(F32) * scale
    s_snk = jnp.broadcast_to(sink.astype(F32)[None, None, :, :, None, None], s_loc.shape[:-1] + (1,))
    p = jax.nn.softmax(jnp.concatenate([s_loc, s_ctx, s_snk], -1), axis=-1)
    p_loc = p[..., :w3].astype(v.dtype)
    p_ctx = p[..., w3:w3 + lc].astype(v.dtype)
    o = (jnp.einsum('bnkgqs,bnskd->bnqkgd', p_loc, vw)
         + jnp.einsum('bnkgqs,bskd->bnqkgd', p_ctx, v_c))
    return o.reshape(B, S, -1)

def fourier_mix(u, f_mix):
    B, L, _ = u.shape
    ug = u.astype(F32).reshape(B, L, F_GROUPS, F_CH)
    z = jnp.fft.fft2(ug, axes=(1, 3), norm='ortho').real.astype(u.dtype)
    return jnp.einsum('blgc,gce->blge', z, f_mix).reshape(B, L, -1)

def retention_scan(q, k, v, log_g, state0):
    Bn, L, H, _ = q.shape
    n = L // RET_CHUNK

    def chunks(t):
        return t.reshape(Bn, n, RET_CHUNK, H, t.shape[-1]).transpose(1, 0, 3, 2, 4)

    idx = jnp.arange(RET_CHUNK, dtype=F32)
    diff = idx[:, None] - idx[None, :]
    decay_in = jnp.where(diff >= 0, jnp.exp(log_g[:, None, None] * jnp.maximum(diff, 0.0)), 0.0)
    xi = jnp.exp(log_g[:, None] * (idx + 1.0))[None, :, :, None]
    zeta = jnp.exp(log_g[:, None] * (RET_CHUNK - 1.0 - idx))[None, :, :, None]
    g_chunk = jnp.exp(log_g * RET_CHUNK)[None, :, None, None]

    def step(state, blk):
        qi, ki, vi = blk
        inner = jnp.einsum('bhqd,bhsd->bhqs', qi, ki) * decay_in
        o = jnp.einsum('bhqs,bhsv->bhqv', inner, vi) + jnp.einsum('bhqd,bhdv->bhqv', qi, state) * xi
        state = state * g_chunk + jnp.einsum('bhsd,bhsv->bhdv', ki * zeta, vi)
        return state, o

    state, o = lax.scan(step, state0, (chunks(q), chunks(k), chunks(v)))
    return o.transpose(1, 0, 3, 2, 4).reshape(Bn, L, H, v.shape[-1]), state

def retention_state(k, v, log_g):
    L = k.shape[1]
    w = jnp.exp(log_g[:, None] * (L - 1.0 - jnp.arange(L, dtype=F32))[None, :])
    return jnp.einsum('blhd,blhv,hl->bhdv', k, v, w)

def bidir_retention(ql, kl, vl, qc, kc, vc, log_g, need_ctx):
    Bn, _, H, dk = ql.shape
    zeros = jnp.zeros((Bn, H, dk, vl.shape[-1]), F32)
    o_l = 0.0
    o_c = 0.0
    for direction in range(2):
        f = (lambda t: t[:, ::-1]) if direction == 1 else (lambda t: t)
        lg = log_g[direction]
        if need_ctx:
            oc, s_ctx = retention_scan(f(qc), f(kc), f(vc), lg, zeros)
            o_c = o_c + f(oc)
        else:
            s_ctx = retention_state(f(kc), f(vc), lg)
        ol, _ = retention_scan(f(ql), f(kl), f(vl), lg, s_ctx)
        o_l = o_l + f(ol)
    return o_l, (o_c if need_ctx else None)

def retention_out(o, g, gn_w):
    mu = jnp.mean(o, -1, keepdims=True)
    var = jnp.mean(jnp.square(o - mu), -1, keepdims=True)
    on = ((o - mu) * lax.rsqrt(var + NORM_EPS)).reshape(o.shape[:2] + (-1,)) * gn_w.astype(F32)
    return (jax.nn.silu(g.astype(F32)) * on).astype(g.dtype)

def swiglu(h, w_gu, w_dn):
    g, u = jnp.split(h @ w_gu, 2, axis=-1)
    return (jax.nn.silu(g) * u) @ w_dn

def mixer(hl, hc, w_in, a_qn, a_kn, b_sink, f_mix, r_decay, r_gn, w_out, grid_tab, seq_tab, need_ctx):
    pl = jnp.split(hl @ w_in, SPLIT_IDX, axis=-1)
    pc = jnp.split(hc @ w_in, SPLIT_IDX, axis=-1)
    qa = rope_2d(rms_norm(heads(pl[0]), a_qn), grid_tab)
    ka = rope_2d(rms_norm(heads(pl[1]), a_kn), grid_tab)
    ka_c = rms_norm(heads(pc[1]), a_kn)
    va, va_c = heads(pl[2]), heads(pc[2])
    a_l = global_attention(group_q(qa, A_KV), jnp.concatenate([ka, ka_c], 1), jnp.concatenate([va, va_c], 1))
    sink = b_sink.reshape(B_KV, B_HEADS // B_KV)
    qb = rope_2d(heads(pl[3]), grid_tab)
    kb = rope_2d(heads(pl[4]), grid_tab)
    kb_c, vb, vb_c = heads(pc[4]), heads(pl[5]), heads(pc[5])
    b_l = window_attention(group_q(qb, B_KV), kb, vb, kb_c, vb_c, sink)
    f_l = fourier_mix(pl[6], f_mix)
    log_g = jax.nn.log_sigmoid(r_decay.astype(F32))
    cos_t, sin_t = seq_tab
    kscale = HEAD_DIM ** -0.5
    qr = rotate(heads(pl[7]), cos_t, sin_t).astype(F32)
    kr = rotate(heads(pl[8]), cos_t, sin_t).astype(F32) * kscale
    o_l, o_c = bidir_retention(qr, kr, heads(pl[9]).astype(F32),
                               heads(pc[7]).astype(F32), heads(pc[8]).astype(F32) * kscale,
                               heads(pc[9]).astype(F32), log_g, need_ctx)
    r_l = retention_out(o_l, pl[10], r_gn)
    y_l = jnp.concatenate([a_l, b_l, f_l, r_l], -1) @ w_out
    if not need_ctx:
        return y_l, None
    a_c = gqa_attend(group_q(rms_norm(heads(pc[0]), a_qn), A_KV), ka_c, va_c, None)
    b_c = gqa_attend(group_q(heads(pc[3]), B_KV), kb_c, vb_c, sink)
    f_c = fourier_mix(pc[6], f_mix)
    r_c = retention_out(o_c, pc[10], r_gn)
    y_c = jnp.concatenate([a_c, b_c, f_c, r_c], -1) @ w_out
    return y_l, y_c

def setup_inputs(seed: int = 0) -> dict:
    key = jax.random.key(seed)
    ks = jax.random.split(key, 20)
    D = D_MODEL

    def nrm(k, shape, s):
        return jax.random.normal(k, shape, F32) * s

    gamma0 = 1.0 - 2.0 ** (-5.0 - jnp.arange(R_HEADS, dtype=F32))
    decay_logit = jnp.log(gamma0 / (1.0 - gamma0))
    return {
        'x': nrm(ks[0], (BATCH, SEQ, D), 1.0),
        'c': nrm(ks[1], (BATCH, D), 1.0),
        'ctx': nrm(ks[2], (BATCH, CTX_LEN, D), 1.0),
        'c_ctx': nrm(ks[3], (D,), 1.0),
        'w_mod': nrm(ks[4], (DEPTH, D, 6 * D), 0.5 * D ** -0.5),
        'b_mod': nrm(ks[5], (DEPTH, 6 * D), 0.02),
        'w_in': nrm(ks[6], (DEPTH, D, IN_W), D ** -0.5),
        'a_q_norm': 1.0 + nrm(ks[7], (DEPTH, HEAD_DIM), 0.02),
        'a_k_norm': 1.0 + nrm(ks[8], (DEPTH, HEAD_DIM), 0.02),
        'b_sink': nrm(ks[9], (DEPTH, B_HEADS), 0.5),
        'f_mix': nrm(ks[10], (DEPTH, F_GROUPS, F_CH, F_CH), F_CH ** -0.5),
        'r_decay': decay_logit[None, None, :] + nrm(ks[11], (DEPTH, 2, R_HEADS), 0.05),
        'r_gn_w': 1.0 + nrm(ks[12], (DEPTH, GROUP_W), 0.02),
        'w_out': nrm(ks[13], (DEPTH, MIX_W, D), BETA * MIX_W ** -0.5),
        'ln1_w': 1.0 + nrm(ks[14], (DEPTH, D), 0.02),
        'ln1_b': nrm(ks[15], (DEPTH, D), 0.02),
        'w_gate_up': nrm(ks[16], (DEPTH, D, 2 * FF_DIM), D ** -0.5),
        'w_down': nrm(ks[17], (DEPTH, FF_DIM, D), BETA * FF_DIM ** -0.5),
        'ln2_w': 1.0 + nrm(ks[18], (DEPTH, D), 0.02),
        'ln2_b': nrm(ks[19], (DEPTH, D), 0.02),
    }

def reference(x, c, ctx, c_ctx, w_mod, b_mod, w_in, a_q_norm, a_k_norm, b_sink, f_mix, r_decay,
              r_gn_w, w_out, ln1_w, ln1_b, w_gate_up, w_down, ln2_w, ln2_b):
    S = x.shape[1]
    rows = S // GRID_W
    t = jnp.arange(rows * GRID_W, dtype=jnp.int32)
    row = (t // GRID_W).astype(F32)
    col = (t % GRID_W).astype(F32)
    axis_freq = HEAD_DIM // 4
    grid_tab = rope_tables(row, axis_freq) + rope_tables(col, axis_freq)
    seq_tab = rope_tables(t.astype(F32), HEAD_DIM // 2)
    for layer in range(DEPTH):
        need_ctx = layer < DEPTH - 1
        mod_l = jax.nn.silu(c) @ w_mod[layer] + b_mod[layer]
        sh1, sc1, g1, sh2, sc2, g2 = [m[:, None, :] for m in jnp.split(mod_l, 6, axis=-1)]
        mod_c = jax.nn.silu(c_ctx) @ w_mod[layer] + b_mod[layer]
        csh1, csc1, cg1, csh2, csc2, cg2 = jnp.split(mod_c, 6, axis=-1)
        y_l, y_c = mixer(modulate(x, sh1, sc1), modulate(ctx, csh1, csc1), w_in[layer],
                         a_q_norm[layer], a_k_norm[layer], b_sink[layer], f_mix[layer], r_decay[layer],
                         r_gn_w[layer], w_out[layer], grid_tab, seq_tab, need_ctx)
        x = post_norm(x, g1 * y_l, ln1_w[layer], ln1_b[layer])
        x = post_norm(x, g2 * swiglu(modulate(x, sh2, sc2), w_gate_up[layer], w_down[layer]),
                      ln2_w[layer], ln2_b[layer])
        if need_ctx:
            ctx = post_norm(ctx, cg1 * y_c, ln1_w[layer], ln1_b[layer])
            ctx = post_norm(ctx, cg2 * swiglu(modulate(ctx, csh2, csc2), w_gate_up[layer], w_down[layer]),
                            ln2_w[layer], ln2_b[layer])
    return x


_drawn_inputs = setup_inputs


def setup_inputs(seed=0):
    import zlib

    import numpy as np

    out = dict(_drawn_inputs(seed))
    spreads = {}
    factors = {'ctx': 3.921,
     'c_ctx': 2.954,
     'b_mod': 5.306,
     'a_q_norm': 33.922,
     'a_k_norm': 29.09,
     'b_sink': 25.64,
     'r_gn_w': 51.831}
    for name, (base, spread) in spreads.items():
        noise = np.random.default_rng([zlib.crc32(name.encode()), seed]).standard_normal(out[name].shape)
        drawn = base * np.exp(spread * noise) if base else spread * noise
        out[name] = __import__('jax').numpy.asarray(drawn.astype(out[name].dtype))
    for name, factor in factors.items():
        out[name] = (out[name] * factor).astype(out[name].dtype)
    return out
```

```python
from contextlib import ExitStack

import numpy as np
import concourse.bass as bass
from concourse import mybir

ALU = mybir.AluOpType
ACT = mybir.ActivationFunctionType
F32 = mybir.dt.float32
R32 = mybir.dt.float32r
AX = mybir.AxisListType.X

P = 128
D = 1024
DEPTH = 2
CTX, SEQ = 256, 512
TOK = CTX + SEQ
NT = TOK // P
CT = CTX // P
HD = 64
FF = 2816
FC = FF // P
HALF = FC // 2
KC = D // P
GRID_W = 64
ALPHA = (2.0 * DEPTH) ** 0.25
EPS = 1e-6
NEG = -1e30
RING = 8
LAT = list(range(CT, NT))
ALL = list(range(NT))

SEGMENTS = {"modA": [0] * 8, "win": [4] * 9, "modB": [0] * 8, "modG": [0] * 4, "wout": [4] * 4, "modC": [0] * 4,
            "gu0": [4] * HALF, "dn0": [4, 4, 3] * 2, "gu1": [4] * HALF, "dn1": [4, 4, 3] * 2}
MOD_BLOCKS = {"modA": [0, 1, 2, 3], "modB": [6, 7, 8, 9], "modG": [4, 5], "modC": [10, 11]}


def plan():
    order = [(0, "modA")]
    for l in range(DEPTH):
        order += [(l, s) for s in ("win", "modB", "modG", "wout", "gu0", "modC", "dn0", "gu1")]
        if l + 1 < DEPTH:
            order.append((l + 1, "modA"))
        order.append((l, "dn1"))
    unit0, slot0, block0, units = {}, {}, {}, []
    slots = mods = blocks = 0
    sent = [0, 0]
    for key in order:
        unit0[key], slot0[key], block0[key] = len(units), slots, blocks
        for n in SEGMENTS[key[1]]:
            slots += n
            mods += n == 0
            sent[len(units) % 2] += 2 if key[1][:2] == "gu" else 1
            units.append((key, n, slots, mods, sent[len(units) % 2]))
        blocks += len(MOD_BLOCKS.get(key[1], ()))
    return order, unit0, slot0, block0, units


ORDER, UNIT0, SLOT0, BLOCK0, UNITS = plan()


def tables():
    f = np.float32
    t = {"ident": np.eye(P, dtype=f)}

    def rot(pos, n):
        inv = (f(10000.0) ** (-np.arange(n, dtype=f) / f(n))).astype(f)
        ang = (pos.astype(f)[:, None] * inv[None, :]).astype(f).astype(np.float64)
        return np.cos(ang), np.sin(ang)

    pos = np.arange(SEQ)
    cr, sr = rot(pos // GRID_W, 16)
    cc, sc = rot(pos % GRID_W, 16)
    cs, ss = rot(pos, 32)
    grid = np.stack([np.concatenate([cr, cr, cc, cc], 1), np.concatenate([-sr, sr, -sc, sc], 1)], 1)
    seq = np.stack([np.concatenate([cs, cs], 1), np.concatenate([-ss, ss], 1)], 1)
    for name, a in (("rope_grid", grid), ("rope_seq", seq)):
        t[name] = a.reshape(SEQ // P, P, 2, HD).transpose(1, 0, 2, 3).astype(f)
    q, j = np.arange(P)[:, None], np.arange(P)[None, :]
    t["mask"] = np.stack([np.where(j >= q, 0, NEG), np.where(j <= q, 0, NEG)], 1).astype(f)
    t["delta"] = (np.arange(-384, 768)[None, :] - q).astype(f)
    a = 2 * np.pi * (np.outer(np.arange(HD), np.arange(HD)) % HD) / HD
    ch = np.zeros((P, 2, P))
    for g in range(2):
        s = slice(g * HD, g * HD + HD)
        ch[s, 0, s] = np.cos(a) / np.sqrt(HD)
        ch[s, 1, s] = -np.sin(a) / np.sqrt(HD)
    t["chan"] = ch.astype(f)
    for name, n in (("dft_lat", SEQ), ("dft_ctx", CTX)):
        a = 2 * np.pi * (np.outer(np.arange(n), np.arange(n)) % n) / n
        m = np.stack([np.cos(a), np.sin(a)], 1) / np.sqrt(n)
        t[name] = m.reshape(n // P, P, 2, n).transpose(1, 0, 2, 3).astype(f)
    t["sel"] = np.array([[1, 0], [0, 1], [1, 1]], f)
    return {k: np.ascontiguousarray(v) for k, v in t.items()}


def build(nc, x, c, ctx_in, c_ctx, w_mod, b_mod, w_in, a_q_norm, a_k_norm, b_sink, f_mix, r_decay,
          r_gn_w, w_out, ln1_w, ln1_b, w_gate_up, w_down, ln2_w, ln2_b, out):
    tab = {k: nc.inline_tensor(v, name="tab_" + k)[tuple(slice(None) for _ in v.shape)] for k, v in tables().items()}
    stack = ExitStack()
    with stack:
        base = (nc.sbuf_base + 63) // 64 * 64
        at = [base]

        def place(name, shape, dt=F32, offset=None):
            size = int(np.prod(shape[1:])) * 4
            if offset is None:
                offset = at[0]
                at[0] += (size + 31) // 32 * 32
            return nc.alloc_sbuf_tensor_at(name, shape, dt, offset=offset)

        X = place("resid", [P, NT, D])
        act_hi = place("act_hi", [P, KC, TOK], R32)
        act_lo = place("act_lo", [P, KC, TOK], R32)
        stage = place("stage", [P, 2, 2048])
        ring_hi = place("ring_hi", [P, RING, 512], R32)
        ring_lo = place("ring_lo", [P, RING, 512], R32)
        PR = at[0]
        at[0] += 62720
        BR = at[0]
        at[0] += 16384
        qk_attn = {"A": place("qk_A", [P, 3, TOK], offset=PR), "B": place("qk_B", [P, 3, TOK], offset=PR + 12288)}
        v_attn = {"A": place("v_A", [P, NT, P], offset=PR + 9216), "B": place("v_B", [P, NT, P], offset=PR + 21504)}
        q_ret = place("q_ret", [P, 2, TOK], offset=PR + 24576)
        k_ret = place("k_ret", [P, 2, TOK], offset=PR + 30720)
        v_ret = place("v_ret", [P, NT, 256], offset=PR + 36864)
        gate_ret = place("gate_ret", [P, NT, 256], offset=PR + 43008)
        u_four = place("u_four", [P, 2, TOK], offset=PR + 49152)
        post = place("post", [P, 2, 512], offset=PR + 55296)
        rope_grid = place("rope_grid", [P, 4, 2, HD], offset=PR + 60160)
        pre = place("pre", [P, NT, 512], offset=BR)
        tmp1 = place("tmp1", [P, 512], offset=BR + 12288)
        tmp2 = place("tmp2", [P, 512], offset=BR + 14336)
        probs = place("probs", [P, 3, TOK], offset=BR)
        probs_T = place("probs_T", [P, 2, TOK], offset=BR + 9216)
        o_attn = place("o_attn", [P, 2, 256], offset=PR + 55296)
        delta = place("delta", [P, 1152], offset=PR + 55296)
        ctx_part = place("ctx_part", [P, 640], offset=PR + 60160)
        strip = place("strip", [P, 2, 896], offset=BR)
        strip_ctx = place("strip_ctx", [P, 2, 640], offset=BR + 7168)
        decayed = place("decayed", [P, 2, 512], offset=BR + 12288)
        dft_lat = place("dft_lat", [P, 4, 2, 512], offset=PR)
        o_ret = place("o_ret", [P, NT, 256], offset=PR + 16384)
        g_mat = place("g_mat", [P, 2, 256], offset=PR + 22528)
        dft_ctx = place("dft_ctx", [P, 2, 2, 256], offset=PR + 24576)
        chan = place("chan", [P, 2, P], offset=PR + 28672)
        mix_bd = place("mix_bd", [P, 2, P], offset=PR + 29696)
        y_ret = place("y_ret", [P, 2, 256], offset=PR + 30720)
        gn_w = place("gn_w", [P, 256], offset=PR + 32768)
        four_ab = place("four_ab", [P, NT, 512], offset=BR)
        hid = place("hid", [P, HALF, TOK], offset=PR)
        silu_g = place("silu_g", [P, 2, TOK], offset=PR + 33792)
        hs_hi = place("hs_hi", [P, 3, TOK], R32, offset=PR + 39936)
        hs_lo = place("hs_lo", [P, 3, TOK], R32, offset=PR + 49152)
        xn = place("xn", [P, 2, D], offset=PR + 39936)
        hbuf = place("hbuf", [P, 2, D], offset=PR + 48128)
        bc = place("bc", [P, 4, D], offset=BR)
        ident = place("ident", [P, P])
        rope_seq = place("rope_seq", [P, 4, 2, HD])
        padded = place("padded", [P, 4, P], offset=at[0] - 2048)
        mask = place("mask", [P, 2, P])
        mod_row = place("mod_row", [3, 2, 512])
        qk_w = place("qk_w", [P, 2, HD])
        st = place("st", [P, NT, 34])
        c_row = place("c_row", [2 * KC, P], offset=PR)
        c_silu = place("c_silu", [P, 2, KC])
        mod_col = place("mod_col", [P, 4, KC, 2])
        ssq = place("ssq", [P, NT, 6])
        rms = place("rms", [P, NT, 6])
        sink = place("sink", [P, 4])
        nsink = place("nsink", [P, 4])
        lg_raw = place("lg_raw", [P, 8])
        lg = place("lg", [P, 3, 4])
        rowmax = place("rowmax", [P, 4])
        negmax = place("negmax", [P, 4])
        expsum = place("expsum", [P, 4])
        expsink = place("expsink", [P, 4])
        rden = place("rden", [P, 4])
        eps = place("eps", [P, 1])
        gst = place("gst", [P, 2, 4, 6])
        gmv = place("gmv", [P, 2, 4, 2])
        gsd = place("gsd", [P, 2, 4])
        grs = place("grs", [P, 2, 4])
        sel = place("sel", [3, 2])
        assert at[0] <= nc.sbuf_usable_end, at[0]

        ps = stack.enter_context(nc.psum_tensor("ps", [P, 8, 512], F32))

        sems = {}

        def sem(*name):
            key = "_".join(str(n) for n in name)
            if key not in sems:
                sems[key] = stack.enter_context(nc.semaphore(key))
            return sems[key]

        x_in, c_in, const_in = sem("x_in"), sem("c_in"), sem("const_in")
        unit_in = [sem("unit_in", 0), sem("unit_in", 1)]
        bias_row_in = [sem("bias_row_in", 0), sem("bias_row_in", 1)]
        w_hi, w_ready, ring_used, mod_used = sem("w_hi"), sem("w_ready"), sem("ring_used"), sem("mod_used")
        mod_row_ready, mod_out, mod_out_read = sem("mod_row_ready"), sem("mod_out"), sem("mod_out_read")
        c_ready = sem("c_ready")
        N_CONST = 5

        def tiles_of(l):
            return ALL if l < DEPTH - 1 else LAT

        def block_tiles(l, b):
            return tiles_of(l) if b in (2, 4) else ALL

        def pre_count(l, b, n):
            return sum(len(block_tiles(l, a)) for a in range(b)) + n + 1

        def unit_wait(e, u):
            e.wait_ge(unit_in[u % 2], 16 * UNITS[u][4])

        def unit_release_wait(e, u):
            _, n, slots, mods, _ = UNITS[u]
            e.wait_ge(w_ready, slots) if n else e.wait_ge(mod_used, mods)

        MOD_KEYS = [(*key, i) for key in ORDER for i in range(len(MOD_BLOCKS.get(key[1], ())))]
        MOD_OUT = {}
        n_out = 0
        for key in ORDER:
            for i, _ in enumerate(MOD_BLOCKS.get(key[1], ())):
                k = 1 if key[1] in ("modA", "modB") else (2 if key[0] < DEPTH - 1 else 1)
                MOD_OUT[(*key, i)] = (n_out, k)
                n_out += k

        def mod_done(l, seg):
            n, k = MOD_OUT[(l, seg, len(MOD_BLOCKS[seg]) - 1)]
            return n + k

        def acc_wait(e, l, seg, p, n, nt, last_slot):
            if n == nt - 1:
                e.wait_ge(ring_used, last_slot + 1)
            else:
                need(e, seg + "_acc", l, p * (nt - 1) + n + 1)

        def win_last_slot(l, b):
            return SLOT0[(l, "win")] + (8 * b + 7 if b < 4 else 35)

        def dn_slot(l, p, j):
            return SLOT0[(l, f"dn{p // 2}")] + (p % 2) * HALF + j

        def hid_slot(p, j):
            if p < 2:
                s = (p * HALF + j) % 3
                return hs_hi[:, s, :], hs_lo[:, s, :]
            s = ((p - 2) * HALF + j) % 8
            return act_hi[:, s, :], act_lo[:, s, :]

        def hid_slot_wait(e, l, p, j):
            n, depth = (p % 2) * HALF + j, 3 if p < 2 else 8
            if n >= depth:
                m = n - depth
                e.wait_ge(ring_used, dn_slot(l, p - p % 2 + m // HALF, m % HALF) + 1)
            elif p >= 2:
                e.wait_ge(ring_used, SLOT0[(l, "dn1")])

        def attn_items(l):
            items = []
            for g in "AB":
                for t in tiles_of(l):
                    if t < CT:
                        keys = [0, 1]
                    elif g == "A":
                        keys = ALL
                    else:
                        keys = [0, 1] + [k for k in (t - 1, t, t + 1) if CT <= k < NT]
                    items += [(g, t, h, keys) for h in range(4)]
            return items

        def ret_items(l):
            items = []
            for h in range(4):
                items += [(h, s, True) for s in ALL]
                if l < DEPTH - 1:
                    items += [(h, s, False) for s in range(CT)]
            return items

        NORMS = [("pre", 0)] + [(l, w) for l in range(DEPTH) for w in (1, 2)]

        def signals(name, l):
            if isinstance(l, tuple):
                if l[0] == "pre":
                    return 0 if name in ("var1", "sd1", "scale1", "normed") else NT
                return len(tiles_of(l[0]))
            nt, blocks = len(tiles_of(l)), [len(block_tiles(l, b)) for b in range(5)]
            n_attn, n_ret, need_ctx = len(attn_items(l)), len(ret_items(l)), l < DEPTH - 1
            return {
                "win_acc": sum(blocks) - 5, "wout_acc": 2 * (nt - 1), "dn_acc": 4 * (nt - 1),
                "pre_ready": sum(blocks), "post_ready": sum(blocks[:4]), "qk_T": sum(blocks[:4]),
                "qk_read": sum(blocks[:4]), "ssq_ready": NT, "rms_sd": NT, "qkw_in": 32 if l == 0 else 64,
                "scores_ready": n_attn, "neg_ready": n_attn, "probs_ready": n_attn, "probs_T_done": n_attn,
                "probs_T_ready": n_attn, "probs_T2_ready": sum(len(i[3]) > 4 for i in attn_items(l)),
                "values_done": n_attn, "o_read": n_attn, "o_T": 2 * nt, "o_hi": 2 * nt, "o_T_lo": 2 * nt,
                "sink_in": 16, "lg_in": 16, "lg_exp": 1, "pad_zero": 1, "q_pad": n_attn, "k_pad": n_ret, "lg_ln": 1, "delta_in": 16,
                "ret_scores": n_ret, "decayed_ready": n_ret, "ret_values": n_ret, "o_ret_ready": 4,
                "strip_arg": 4, "strip_exp": 12, "strip_ready": 4,
                "four_in": 16 * (7 if need_ctx else 6), "gn_in": 16, "mix_zero": 1, "g_done": 1, "g_ready": 1,
                "ab_done": nt, "ab_ready": nt, "gvar": nt, "gsd": nt, "y_ret_ready": nt, "y_T": nt, "y_hi": nt,
                "y_lo": nt, "four_done": 4 if need_ctx else 2, "four_hi": 4 if need_ctx else 2,
                "four_lo": 4 if need_ctx else 2, "norm_in": 64, "silu_ready": 2 * HALF, "hid_ready": 2 * HALF,
                "hid_hi": 4 * HALF, "hid_split": 4 * HALF, "wout_read": 2 * nt, "dn_read": 4 * nt,
            }[name]

        def need(e, name, l, n):
            before = NORMS[:NORMS.index(l)] if isinstance(l, tuple) else range(l)
            e.wait_ge(sem(name), n + sum(signals(name, k) for k in before))

        block = stack.enter_context(nc.Block())

        @block.sync
        def _(sp):
            def send(u, src):
                if u >= 2:
                    unit_release_wait(sp, u - 2)
                sp.dma_start(stage[:, u % 2, 0:src[1]].rearrange(src[2], **src[3]), src[0]).then_inc(unit_in[u % 2], 16)

            def rows(w, k0, n, c0, width):
                return (w[k0 * P:(k0 + n) * P, c0:c0 + width].rearrange("(k p) c -> p k c", p=P), n * width,
                        "p (k c) -> p k c", {"k": n})

            def gu_src(l, h, f):
                return w_gate_up[l, :, h * FF:(h + 1) * FF].rearrange("(k p) c -> p k c", p=P)[:, :, bass.ds(f * P, P)]

            for l, seg in ORDER:
                u0 = UNIT0[(l, seg)]
                if seg in MOD_BLOCKS:
                    for i, b in enumerate(MOD_BLOCKS[seg]):
                        m = BLOCK0[(l, seg)] + i
                        if m >= 2:
                            sp.wait_ge(mod_out, sum(MOD_OUT[MOD_KEYS[m - 2]]))
                        sp.dma_start(mod_row[2:3, m % 2, :], b_mod[l:l + 1, b * 512:(b + 1) * 512]).then_inc(bias_row_in[m % 2], 16)
                        for h in range(2):
                            send(u0 + 2 * i + h, rows(w_mod[l], 4 * h, 4, b * 512, 512))
                elif seg == "win":
                    for b in range(4):
                        for h in range(2):
                            send(u0 + 2 * b + h, rows(w_in[l], 4 * h, 4, b * 512, 512))
                    send(u0 + 8, rows(w_in[l], 0, 8, 2048, 256))
                elif seg == "wout":
                    for i in range(4):
                        send(u0 + i, rows(w_out[l], 4 * (i % 2), 4, (i // 2) * 512, 512))
                elif seg[:2] == "gu":
                    f0 = HALF * int(seg[2])
                    dst = [stage[:, q, :].rearrange("p (k g c) -> p k g c", k=KC, g=2) for q in range(2)]

                    def send_gu(e, f):
                        for h in range(2):
                            sp.dma_start(dst[(u0 + e) % 2][:, :, h, :], gu_src(l, h, f)).then_inc(unit_in[(u0 + e) % 2], 16)

                    for g in range(2):
                        unit_release_wait(sp, u0 + g - 2)
                        send_gu(g, f0 + g)
                    with sp.Fori(1, HALF // 2) as i:
                        for e in range(2):
                            sp.wait_ge(w_ready, i * 8 + (SLOT0[(l, seg)] - 8 + 4 * (e + 1)))
                            send_gu(e, i * 2 + (f0 + e))
                    unit_release_wait(sp, u0 + HALF - 3)
                    send_gu(HALF - 1, f0 + HALF - 1)
                else:
                    f0 = HALF * int(seg[2])
                    for i in range(6):
                        k0 = f0 + 4 * (i % 3)
                        send(u0 + i, rows(w_down[l], k0, SEGMENTS[seg][i], (i // 3) * 512, 512))

            for n, t in enumerate(LAT):
                sp.wait_ge(sem("x_ready"), n + 1)
                sp.dma_start(out[0, (t - CT) * P:(t - CT + 1) * P, :], X[:, t, :]).then_inc(sem("out_sent"), 16)
            sp.wait_ge(sem("out_sent"), 16 * len(LAT))

        @block.gpsimd
        def _(pool):
            def split(g, par, j, n_hi):
                nc.gpsimd.tensor_scalar(ring_hi[:, g % RING, :], stage[:, par, j * 512:(j + 1) * 512], 1.0, 0.0,
                                        ALU.mult, ALU.add).then_inc(w_hi, 1)
                pool.wait_ge(w_hi, n_hi)
                nc.gpsimd.tensor_tensor(ring_lo[:, g % RING, :], stage[:, par, j * 512:(j + 1) * 512],
                                        ring_hi[:, g % RING, :].bitcast(F32), ALU.subtract).then_inc(w_ready, 1)

            def pads(l):
                items, rets = attn_items(l), ret_items(l)
                need(pool, "qk_read", l, sum(len(block_tiles(l, b)) for b in range(4)))
                for a in range(2):
                    other = slice((1 - a) * HD, (1 - a) * HD + HD)
                    z = nc.gpsimd.memset(padded[other, 2 * a:2 * a + 2, :], 0.0)
                z.then_inc(sem("pad_zero"), 1)
                need(pool, "pad_zero", l, 1)
                for i, (g, t, h, _) in enumerate(items):
                    rows = slice((h // 2) * HD, (h // 2) * HD + HD)
                    if i >= 4:
                        need(pool, "scores_ready", l, i - 3)
                    nc.gpsimd.tensor_scalar(padded[rows, h, :], qk_attn[g][rows, h % 2, t * P:(t + 1) * P], 1.0, 0.0,
                                            ALU.mult, ALU.add).then_inc(sem("q_pad"), 1)
                need(pool, "scores_ready", l, len(items))
                for i, (h, s, _) in enumerate(rets):
                    rows = slice((h % 2) * HD, (h % 2) * HD + HD)
                    if i >= 2:
                        need(pool, "ret_scores", l, i - 1)
                    nc.gpsimd.tensor_scalar(padded[rows, 2 * (h % 2) + i % 2, :], k_ret[rows, h // 2, s * P:(s + 1) * P],
                                            1.0, 0.0, ALU.mult, ALU.add).then_inc(sem("k_pad"), 1)

            for l, seg in ORDER:
                u0, g0 = UNIT0[(l, seg)], SLOT0[(l, seg)]
                if seg == "modB":
                    pads(l)
                if seg in MOD_BLOCKS:
                    continue
                for n in SEGMENTS[seg]:
                    unit_wait(pool, u0)
                    for j in range(n):
                        if g0 >= RING:
                            pool.wait_ge(ring_used, g0 - 7)
                        split(g0, u0 % 2, j, g0 + 1)
                        g0 += 1
                    u0 += 1

        @block.tensor
        def _(pe):
            def product(o, a_hi, a_lo, b_hi, b_lo, first, last):
                nc.tensor.matmul(o, a_hi, b_hi, start=first, stop=False)
                nc.tensor.matmul(o, a_hi, b_lo, start=False, stop=False)
                return nc.tensor.matmul(o, a_lo, b_hi, start=False, stop=last)

            def mod_segment(l, seg):
                for i, b in enumerate(MOD_BLOCKS[seg]):
                    m = BLOCK0[(l, seg)] + i
                    if m >= 2:
                        pe.wait_ge(mod_row_ready, m - 1)
                    for h in range(2):
                        u = UNIT0[(l, seg)] + 2 * i + h
                        unit_wait(pe, u)
                        for k in range(4):
                            mm = nc.tensor.matmul(ps[0:2, m % 2, :], c_silu[:, :, 4 * h + k],
                                                  stage[:, u % 2, k * 512:(k + 1) * 512],
                                                  start=(4 * h + k == 0), stop=(4 * h + k == 7))
                        mm.then_inc(mod_used, 1)
                    pe.wait_ge(mod_row_ready, m + 1)
                    pe.wait_ge(bias_row_in[m % 2], 16 * (m // 2 + 1))
                    n, k = MOD_OUT[(l, seg, i)]
                    for o in range(k):
                        if n + o >= 2:
                            pe.wait_ge(mod_out_read, n + o - 1)
                        bank = 2 + (n + o) % 2
                        if seg in ("modA", "modB"):
                            for q in range(4):
                                mm = nc.tensor.matmul(ps[:, bank, 2 * q:2 * q + 2], mod_row[:, m % 2, q * P:(q + 1) * P],
                                                      sel[:, 0:2], start=True, stop=True)
                        else:
                            mm = nc.tensor.matmul(ps[:, bank, :], sel[:, o:o + 1].to_broadcast([3, P]), mod_row[:, m % 2, :],
                                                  start=True, stop=True)
                        mm.then_inc(mod_out, 1)

            def transposes(key, n):
                need(pe, "xn_ready", key, n + 1)
                if n > 0:
                    need(pe, "h_ready", key, n)
                for k in range(KC):
                    mm = nc.tensor.transpose(ps[:, 6 + k // 4, (k % 4) * P:(k % 4 + 1) * P], xn[:, n % 2, k * P:(k + 1) * P],
                                             ident[:, :])
                mm.then_inc(sem("xn_T"), 1)

            def project(l):
                g = SLOT0[(l, "win")]
                key = ("pre", 0) if l == 0 else (l - 1, 2)
                tp = [0]

                def tpose(b, n, t):
                    nc_ = {0: 3, 1: 3, 2: 4, 3: 2}[b]
                    need(pe, "post_ready", l, pre_count(l, b, n))
                    if tp[0] >= 2:
                        need(pe, "qk_read", l, tp[0] - 1)
                    for k in range(nc_):
                        src = post[:, tp[0] % 2, k * P:(k + 1) * P]
                        mm = nc.tensor.transpose(ps[:, 6 + tp[0] % 2, k * P:(k + 1) * P], src, ident[:, :])
                    mm.then_inc(sem("qk_T"), 1)
                    tp[0] += 1

                for b in range(5):
                    tiles = block_tiles(l, b)
                    width, ks, slots = (512, 1, 8) if b < 4 else (256, 2, 4)
                    for j in range(slots):
                        pe.wait_ge(w_ready, g + 1)
                        for n, t in enumerate(tiles):
                            if j == 0 and b == 0:
                                need(pe, "act_ready", key, n + 1)
                            elif j == 0:
                                pb = block_tiles(l, b - 1)
                                if t in pb:
                                    need(pe, "pre_ready", l, pre_count(l, b - 1, pb.index(t)))
                                else:
                                    pb = block_tiles(l, b - 2)
                                    need(pe, "pre_ready", l, pre_count(l, b - 2, pb.index(t)))
                            for q in range(ks):
                                k = ks * j + q
                                s = slice(t * P, (t + 1) * P)
                                w = slice(q * width, (q + 1) * width)
                                mm = product(ps[:, t, 0:width], act_hi[:, k, s], act_lo[:, k, s],
                                             ring_hi[:, g % RING, w], ring_lo[:, g % RING, w], k == 0, k == KC - 1)
                            if n == len(tiles) - 1:
                                mm.then_inc(ring_used, 1)
                            elif j == slots - 1:
                                mm.then_inc(sem("win_acc"), 1)
                        g += 1
                        if 0 < b < 4 and j >= 2:
                            pt = block_tiles(l, b - 1)
                            if j - 2 < len(pt):
                                tpose(b - 1, j - 2, pt[j - 2])
                for n, t in enumerate(block_tiles(l, 3)):
                    tpose(3, n, t)

            def attention(l):
                items = attn_items(l)
                tiles = tiles_of(l)
                total = len(items)

                def scores(i):
                    g, t, h, keys = items[i]
                    q = padded[:, h, :]
                    kT = qk_attn[g]
                    need(pe, "q_pad", l, i + 1)
                    bank = 2 * (i % 2)
                    if i >= 2:
                        need(pe, "probs_ready", l, i - 1)
                    runs, col = [], 0
                    for k in keys:
                        if runs and runs[-1][1] + runs[-1][2] == k and (col // 512 == runs[-1][0] // 512):
                            runs[-1][2] += 1
                        else:
                            runs.append([col, k, 1])
                        col += P
                    flat = ps[:, bank:bank + 2, :].rearrange("p b n -> p (b n)")
                    for r, (c0, k0, m) in enumerate(runs):
                        edge = g == "B" and t >= CT
                        masks = [(kk, 0 if kk < t else 1) for kk in range(k0, k0 + m) if edge and kk >= CT and kk != t]
                        mm = nc.tensor.matmul(flat[:, c0:c0 + m * P], q, kT[:, 2, k0 * P:(k0 + m) * P],
                                              start=True, stop=not masks, skip_group_check=True)
                        for a, (kk, which) in enumerate(masks):
                            o = c0 + (kk - k0) * P
                            mm = nc.tensor.matmul(flat[:, o:o + P], ident[:, :], mask[:, which, :],
                                                  start=False, stop=(a == len(masks) - 1), skip_group_check=True)
                    mm.then_inc(sem("scores_ready"), 1)

                def transpose_probs(i):
                    _, _, _, keys = items[i]
                    need(pe, "probs_ready", l, i + 1)
                    if i >= 1:
                        need(pe, "probs_T_ready", l, i)
                        n = sum(len(items[a][3]) > 4 for a in range(i))
                        if n:
                            need(pe, "probs_T2_ready", l, n)
                    flat = ps[:, 4:6, :].rearrange("p b n -> p (b n)")
                    for k in range(len(keys)):
                        mm = nc.tensor.transpose(flat[:, k * P:(k + 1) * P], probs[:, i % 3, k * P:(k + 1) * P], ident[:, :])
                    mm.then_inc(sem("probs_T_done"), 1)

                def values(i):
                    g, t, h, keys = items[i]
                    need(pe, "probs_T_ready", l, i + 1)
                    n = sum(len(items[a][3]) > 4 for a in range(i + 1))
                    if n:
                        need(pe, "probs_T2_ready", l, n)
                    if i >= 2:
                        need(pe, "o_read", l, i - 1)
                    for a, k in enumerate(keys):
                        mm = nc.tensor.matmul(ps[:, 6 + i % 2, 0:HD], probs_T[:, i % 2, a * P:(a + 1) * P],
                                              v_attn[g][:, k, (h // 2) * HD:(h // 2 + 1) * HD],
                                              start=(a == 0), stop=(a == len(keys) - 1))
                    mm.then_inc(sem("values_done"), 1)

                def out_T(q):
                    need(pe, "o_read", l, 4 * q + 4)
                    for k in range(2):
                        mm = nc.tensor.transpose(ps[:, 7, 256 + k * P:256 + (k + 1) * P], o_attn[:, q % 2, k * P:(k + 1) * P], ident[:, :])
                    mm.then_inc(sem("o_T"), 1)

                for s in range(total + 5):
                    if s < total:
                        scores(s)
                    if 2 <= s < total + 2:
                        transpose_probs(s - 2)
                    if 3 <= s < total + 3:
                        i = s - 3
                        if i % 2 and i >= 5:
                            need(pe, "o_T_lo", l, (i - 1) // 4)
                        values(i)
                    if s >= 4 and (s - 4) % 4 == 3 and s - 4 < total:
                        out_T((s - 4) // 4)

            def retention(l):
                items = ret_items(l)
                per = len(items) // 4
                need_ctx = l < DEPTH - 1
                n_t = len(tiles_of(l))

                def scores(i):
                    h, s, lat = items[i]
                    cols = slice(CTX, TOK) if lat else slice(0, CTX)
                    need(pe, "k_pad", l, i + 1)
                    if i >= 2:
                        need(pe, "decayed_ready", l, i - 1)
                    elif i == 0:
                        need(pe, "probs_ready", l, len(attn_items(l)))
                    mm = nc.tensor.matmul(ps[:, i % 2, 0:cols.stop - cols.start], padded[:, 2 * (h % 2) + i % 2, :],
                                          q_ret[:, h // 2, cols], start=True, stop=True)
                    mm.then_inc(sem("ret_scores"), 1)

                def values(i):
                    h, s, lat = items[i]
                    need(pe, "decayed_ready", l, i + 1)
                    first = i % per == 0
                    if first and h >= 2:
                        need(pe, "o_ret_ready", l, h - 1)
                    queries = range(4) if lat else range(2)
                    for a in queries:
                        col = (a if lat else 4 + a) * HD
                        mm = nc.tensor.matmul(ps[:, 2 + h % 2, col:col + HD], decayed[:, i % 2, a * P:(a + 1) * P],
                                              v_ret[:, s, h * HD:(h + 1) * HD], start=(first and a == 0),
                                              stop=(i % per == per - 1 and a == queries[-1]), skip_group_check=True)
                    mm.then_inc(sem("ret_values"), 1)

                for s in range(len(items) + 2):
                    if s < len(items):
                        scores(s)
                    if s >= 2:
                        values(s - 2)

            def fourier(l):
                need_ctx = l < DEPTH - 1
                tiles = tiles_of(l)
                need(pe, "four_in", l, 16 * (7 if need_ctx else 6))
                need(pe, "o_T_lo", l, len(tiles) * 2)
                for ch in range(2):
                    for w in range(2):
                        mm = nc.tensor.matmul(ps[:, 4, ch * 256 + w * P:ch * 256 + (w + 1) * P], chan[:, w, :], mix_bd[:, ch, :],
                                              start=True, stop=True)
                mm.then_inc(sem("g_done"), 1)
                need(pe, "g_ready", l, 1)
                for n, t in enumerate(tiles):
                    if n >= 2:
                        need(pe, "ab_ready", l, n - 1)
                    for ch in range(2):
                        mm = nc.tensor.matmul(ps[:, 4 + (n + 1) % 2, ch * 256:(ch + 1) * 256], u_four[:, ch, t * P:(t + 1) * P],
                                              g_mat[:, ch, :], start=True, stop=True)
                    mm.then_inc(sem("ab_done"), 1)
                need(pe, "ab_ready", l, len(tiles))
                need(pe, "decayed_ready", l, len(ret_items(l)))
                for ch in range(2):
                    n = 0
                    for t in LAT:
                        for w in range(2):
                            o = ch * 256 + w * P
                            mm = nc.tensor.matmul(ps[:, 6 + ch, :], four_ab[:, t, o:o + P], dft_lat[:, t - CT, w, :],
                                                  start=(n == 0), stop=(n == 7))
                            n += 1
                    mm.then_inc(sem("four_done"), 1)
                if need_ctx:
                    for ch in range(2):
                        n = 0
                        for t in range(CT):
                            for w in range(2):
                                o = ch * 256 + w * P
                                mm = nc.tensor.matmul(ps[:, ch, 0:CTX], four_ab[:, t, o:o + P], dft_ctx[:, t, w, :],
                                                      start=(n == 0), stop=(n == 3))
                                n += 1
                        mm.then_inc(sem("four_done"), 1)
                for n, t in enumerate(tiles):
                    need(pe, "y_ret_ready", l, n + 1)
                    if n >= 2:
                        need(pe, "y_lo", l, n - 1)
                    for k in range(2):
                        mm = nc.tensor.transpose(ps[:, 4 + n % 2, k * P:(k + 1) * P], y_ret[:, n % 2, k * P:(k + 1) * P], ident[:, :])
                    mm.then_inc(sem("y_T"), 1)

            def mix_out(l):
                tiles = tiles_of(l)
                nt = len(tiles)
                key = (l, 1)
                g = SLOT0[(l, "wout")]
                need(pe, "y_lo", l, nt)
                need(pe, "four_lo", l, 4 if l < DEPTH - 1 else 2)
                pe.wait_ge(mod_out_read, mod_done(l, "modG"))
                for j in range(8):
                    pe.wait_ge(w_ready, g + 1)
                    for n, t in enumerate(tiles):
                        s = slice(t * P, (t + 1) * P)
                        mm = product(ps[:, t, :], act_hi[:, j, s], act_lo[:, j, s], ring_hi[:, g % RING, :],
                                     ring_lo[:, g % RING, :], j == 0, j == 7)
                        if n == nt - 1:
                            mm.then_inc(ring_used, 1)
                        elif j == 7:
                            mm.then_inc(sem("wout_acc"), 1)
                    g += 1
                last_pass(l, key, tiles, "wout", 1, g, 8, lambda j, s: (act_hi[:, j, s], act_lo[:, j, s]), None)

            def last_pass(l, key, tiles, seg, p, g, m, left, ready):
                nt = len(tiles)
                for n, t in enumerate(tiles):
                    s = slice(t * P, (t + 1) * P)
                    if m == 8:
                        need(pe, seg + "_read", l, (p - 1) * nt + n + 1)
                    for j in range(8):
                        if n == 0:
                            pe.wait_ge(w_ready, g + j + 1)
                            if ready:
                                ready(j)
                        a_hi, a_lo = left(j, s)
                        mm = product(ps[:, t, :], a_hi, a_lo, ring_hi[:, (g + j) % RING, :],
                                     ring_lo[:, (g + j) % RING, :], j == 0 and m == 8, j == 7)
                        if n == nt - 1:
                            mm.then_inc(ring_used, 1)
                        elif j == 7:
                            mm.then_inc(sem(seg + "_acc"), 1)
                    if n >= 4 and key != (DEPTH - 1, 2):
                        transposes(key, n - 4)
                if key != (DEPTH - 1, 2):
                    for n in range(max(nt - 4, 0), nt):
                        transposes(key, n)

            def gate_up(l, fh):
                lo_col, width, parts = (0, 384, 2) if l < DEPTH - 1 else (CTX, 512, 1)
                seg = f"gu{fh}"
                g0 = SLOT0[(l, seg)]
                f0 = fh * HALF

                def chunk(g, f, i, slot_base, hid_base, first_pair):
                    bank = 4 * (f % 2)
                    if not first_pair:
                        need(pe, "hid_ready", l, hid_base)
                    for j in range(4):
                        pe.wait_ge(w_ready, slot_base + j)
                        for q in range(2):
                            k = 2 * j + q
                            for gu in range(2):
                                w = slice(q * 256 + gu * P, q * 256 + (gu + 1) * P)
                                wh, wl = ring_hi[:, (g + j) % RING, w], ring_lo[:, (g + j) % RING, w]
                                for r in range(parts):
                                    o = ps[:, bank + 2 * gu + r, 0:width]
                                    s = slice(lo_col + r * width, lo_col + (r + 1) * width)
                                    mm = product(o, wh, wl, act_hi[:, k, s], act_lo[:, k, s], k == 0, k == 7)
                        mm.then_inc(ring_used, 1)

                if fh == 0:
                    need(pe, "act_ready", (l, 1), len(tiles_of(l)))
                else:
                    need(pe, "dn_read", l, 2 * len(tiles_of(l)))
                for f in range(2):
                    chunk(g0 + 4 * f, f, None, g0 + 4 * f + 1, None, True)
                with pe.Fori(1, HALF // 2) as i:
                    for e in range(2):
                        chunk(g0 + 4 * e, e, i, i * 8 + (g0 + 4 * e + 1), i * 2 + (f0 + e - 1), False)
                f = HALF - 1
                chunk(g0 + 4 * f, f, None, g0 + 4 * f + 1, f0 + f - 1, False)

            def down(l, fh):
                tiles = tiles_of(l)
                nt = len(tiles)
                for dh in range(2):
                    p = 2 * fh + dh
                    n_outer = 3 if p == 3 else HALF
                    for j in range(n_outer):
                        g = dn_slot(l, p, j)
                        pe.wait_ge(w_ready, g + 1)
                        need(pe, "hid_split", l, p * HALF + j + 1)
                        a_hi, a_lo = hid_slot(p, j)
                        for n, t in enumerate(tiles):
                            if j == 0:
                                if dh == 0:
                                    need(pe, "hid_ready", l, (fh + 1) * HALF)
                                else:
                                    need(pe, "dn_read", l, (p - 1) * nt + n + 1)
                            s = slice(t * P, (t + 1) * P)
                            mm = product(ps[:, t, :], a_hi[:, s], a_lo[:, s], ring_hi[:, g % RING, :],
                                         ring_lo[:, g % RING, :], j == 0, j == HALF - 1)
                            if n == nt - 1:
                                mm.then_inc(ring_used, 1)
                            elif j == HALF - 1:
                                mm.then_inc(sem("dn_acc"), 1)
                    if p == 3:
                        last_pass(l, (l, 2), tiles, "dn", 3, dn_slot(l, 3, 3), 11,
                                  lambda j, s: tuple(h[:, s] for h in hid_slot(3, 3 + j)),
                                  lambda j: need(pe, "hid_split", l, 3 * HALF + 3 + j + 1))

            pe.wait_ge(const_in, 16 * N_CONST)
            pe.wait_ge(sem("c_row_ready"), 1)
            nc.tensor.transpose(ps[:, 0, 0:2 * KC], c_row[:, :], ident[0:2 * KC, 0:2 * KC]).then_inc(sem("c_T"), 1)
            pe.wait_ge(c_ready, 1)
            mod_segment(0, "modA")
            for n in range(NT):
                transposes(("pre", 0), n)
            for l in range(DEPTH):
                tiles = tiles_of(l)
                project(l)
                need(pe, "pre_ready", l, pre_count(l, 4, len(tiles) - 1))
                mod_segment(l, "modB")
                pe.wait_ge(mod_out_read, mod_done(l, "modB"))
                need(pe, "qk_read", l, sum(len(block_tiles(l, b)) for b in range(4)))
                attention(l)
                retention(l)
                fourier(l)
                need(pe, "four_lo", l, 4 if l < DEPTH - 1 else 2)
                need(pe, "o_ret_ready", l, 4)
                mod_segment(l, "modG")
                mix_out(l)
                gate_up(l, 0)
                need(pe, "hid_ready", l, HALF)
                mod_segment(l, "modC")
                pe.wait_ge(mod_out_read, mod_done(l, "modC"))
                down(l, 0)
                gate_up(l, 1)
                if l < DEPTH - 1:
                    need(pe, "hid_ready", l, 2 * HALF)
                    mod_segment(l + 1, "modA")
                    pe.wait_ge(mod_out_read, mod_done(l + 1, "modA"))
                down(l, 1)

        @block.scalar
        def _(act):
            a = nc.scalar

            def mod_segment(l, seg):
                for i, b in enumerate(MOD_BLOCKS[seg]):
                    m = BLOCK0[(l, seg)] + i
                    n, k = MOD_OUT[(l, seg, i)]
                    if m >= 2:
                        act.wait_ge(mod_out, sum(MOD_OUT[MOD_KEYS[m - 2]]))
                    act.wait_ge(mod_used, 2 * (m + 1))
                    a.activation(mod_row[0:2, m % 2, :], ps[0:2, m % 2, :], ACT.Copy).then_inc(mod_row_ready, 1)
                    for o in range(k):
                        act.wait_ge(mod_out, n + o + 1)
                        bank = 2 + (n + o) % 2
                        if seg in ("modA", "modB"):
                            which = b // 2 if seg == "modA" else b // 2 - 1
                            dst = mod_col[:, which, 4 * (b % 2):4 * (b % 2) + 4, :]
                            a.activation(dst, ps[:, bank, 0:8].rearrange("p (k s) -> p k s", s=2), ACT.Copy).then_inc(mod_out_read, 1)
                        else:
                            a.activation(bc[:, o, (b % 2) * 512:(b % 2 + 1) * 512], ps[:, bank, :], ACT.Copy).then_inc(mod_out_read, 1)

            def norm_steps(key, tiles, post_norm):
                last = key == (DEPTH - 1, 2)
                nt = len(tiles)
                for step in range(nt + 5):
                    for s in (4, 3, 2, 1, 0):
                        n = step - s
                        if not 0 <= n < nt:
                            continue
                        t = tiles[n]
                        if s == 0 and post_norm:
                            need(act, "var1", key, n + 1)
                            a.activation(st[:, t, 14:15], st[:, t, 13:14], ACT.Sqrt, bias=eps[:, :]).then_inc(sem("sd1"), 1)
                        elif s == 1 and post_norm:
                            need(act, "scale1", key, n + 1)
                            a.activation(X[:, t, :], X[:, t, :], ACT.Identity, bias=st[:, t, 16:17],
                                         scale=st[:, t, 15:16]).then_inc(sem("normed"), 1)
                        elif s == 2 and not last:
                            need(act, "var2", key, n + 1)
                            a.activation(st[:, t, 31:32], st[:, t, 30:31], ACT.Sqrt, bias=eps[:, :]).then_inc(sem("sd2"), 1)
                        elif s == 3 and not last:
                            need(act, "scale2", key, n + 1)
                            if n >= 2:
                                need(act, "xn_T", key, n - 1)
                            a.activation(xn[:, n % 2, :], X[:, t, :], ACT.Identity, bias=st[:, t, 33:34],
                                         scale=st[:, t, 32:33]).then_inc(sem("xn_ready"), 1)
                        elif s == 4 and not last:
                            need(act, "h_ready", key, n + 1)
                            a.activation(act_hi[:, :, t * P:(t + 1) * P], hbuf[:, n % 2, :].rearrange("p (k t) -> p k t", k=KC),
                                         ACT.Copy).then_inc(sem("h_hi"), 1)

            def project(l):
                tp = [0]

                def read_T(b, n, t):
                    need(act, "qk_T", l, tp[0] + 1)
                    src = ps[:, 6 + tp[0] % 2, :].rearrange("p (k t) -> p k t", t=P)
                    s = slice(t * P, (t + 1) * P)
                    if b < 2:
                        ins = a.activation(qk_attn["AB"[b]][:, :, s], src[:, 0:3, :], ACT.Copy)
                    elif b == 2:
                        a.activation(u_four[:, :, s], src[:, 0:2, :], ACT.Copy)
                        ins = a.activation(q_ret[:, :, s], src[:, 2:4, :], ACT.Copy)
                    else:
                        ins = a.activation(k_ret[:, :, s], src[:, 0:2, :], ACT.Copy)
                    ins.then_inc(sem("qk_read"), 1)
                    tp[0] += 1

                for b in range(5):
                    if 0 < b < 4:
                        if b == 1:
                            for n, t in enumerate(ALL):
                                need(act, "ssq_ready", l, n + 1)
                                a.activation(rms[:, t, :], ssq[:, t, :], ACT.Sqrt, bias=eps[:, :], scale=1.0 / HD).then_inc(sem("rms_sd"), 1)
                        for n, t in enumerate(block_tiles(l, b - 1)):
                            read_T(b - 1, n, t)
                    tiles = block_tiles(l, b)
                    for n, t in enumerate(tiles):
                        if n == len(tiles) - 1:
                            act.wait_ge(ring_used, win_last_slot(l, b) + 1)
                        else:
                            need(act, "win_acc", l, sum(len(block_tiles(l, q)) - 1 for q in range(b)) + n + 1)
                        if 0 < b < 4:
                            need(act, "post_ready", l, pre_count(l, b - 1, len(block_tiles(l, b - 1)) - 1))
                        acc = ps[:, t, :]
                        if b < 2:
                            a.activation(v_attn["AB"[b]][:, t, :], acc[:, 384:512], ACT.Copy)
                            ins = a.activation(pre[:, t, 0:384], acc[:, 0:384], ACT.Copy)
                        elif b == 2:
                            ins = a.activation(pre[:, t, :], acc, ACT.Copy)
                        elif b == 3:
                            a.activation(v_ret[:, t, :], acc[:, 256:512], ACT.Copy)
                            ins = a.activation(pre[:, t, 0:256], acc[:, 0:256], ACT.Copy)
                        else:
                            ins = a.activation(gate_ret[:, t, :], acc[:, 0:256], ACT.Silu)
                        ins.then_inc(sem("pre_ready"), 1)
                for n, t in enumerate(block_tiles(l, 3)):
                    read_T(3, n, t)

            def attention(l):
                items = attn_items(l)
                total = len(items)

                def probabilities(i):
                    g, t, h, keys = items[i]
                    n = len(keys) * P
                    need(act, "neg_ready", l, i + 1)
                    if i >= 3:
                        need(act, "probs_T_done", l, i - 2)
                    flat = ps[:, 2 * (i % 2):2 * (i % 2) + 2, :].rearrange("p b n -> p (b n)")
                    if g == "B":
                        a.activation(expsink[:, i % 4:i % 4 + 1], negmax[:, i % 4:i % 4 + 1], ACT.Exp, bias=sink[:, h:h + 1])
                    a.activation(probs[:, i % 3, 0:n], flat[:, 0:n], ACT.Exp, bias=negmax[:, i % 4:i % 4 + 1], scale=0.125,
                                 accum_out=expsum[:, i % 4:i % 4 + 1]).then_inc(sem("probs_ready"), 1)

                def read_T2(i):
                    g, t, h, keys = items[i]
                    if len(keys) <= 4:
                        return
                    need(act, "probs_T_done", l, i + 1)
                    if i >= 2:
                        need(act, "values_done", l, i - 1)
                    n = (len(keys) - 4) * P
                    a.activation(probs_T[:, i % 2, 512:512 + n], ps[:, 5, 0:n], ACT.Copy).then_inc(sem("probs_T2_ready"), 1)

                def out_hi(q):
                    g, t, _, _ = items[4 * q]
                    need(act, "o_T", l, q + 1)
                    ch = 0 if g == "A" else 2
                    a.activation(act_hi[:, ch:ch + 2, t * P:(t + 1) * P], ps[:, 7, 256:512].rearrange("p (k t) -> p k t", t=P),
                                 ACT.Copy).then_inc(sem("o_hi"), 1)

                for s in range(total + 5):
                    if s < total:
                        probabilities(s)
                    if 2 <= s < total + 2:
                        read_T2(s - 2)
                    if s >= 4 and (s - 4) % 4 == 3 and s - 4 < total:
                        out_hi((s - 4) // 4)

            def retention(l):
                items = ret_items(l)
                per = len(items) // 4
                need_ctx = l < DEPTH - 1
                need(act, "lg_in", l, 16)
                a.activation(lg_raw[:, :], lg_raw[:, :], ACT.Exp, scale=-1.0).then_inc(sem("lg_exp"), 1)
                need(act, "lg_exp", l, 1)
                a.activation(lg_raw[:, :], lg_raw[:, :], ACT.Ln, bias=1.0).then_inc(sem("lg_ln"), 1)

                def strips(h):
                    if h >= 2:
                        need(act, "decayed_ready", l, per * (h - 1))
                    need(act, "strip_arg", l, h + 1)
                    a.activation(strip[:, h % 2, :], strip[:, h % 2, :], ACT.Exp).then_inc(sem("strip_exp"), 1)
                    a.activation(strip_ctx[:, h % 2, :], delta[:, 512:1152], ACT.Exp, scale=lg[:, 0, h:h + 1]).then_inc(sem("strip_exp"), 1)
                    if h >= 1:
                        need(act, "strip_ready", l, h)
                    a.activation(ctx_part[:, :], delta[:, 384:1024], ACT.Exp, scale=lg[:, 1, h:h + 1],
                                 bias=lg[:, 2, h:h + 1]).then_inc(sem("strip_exp"), 1)

                def head_out(h):
                    need(act, "ret_values", l, per * (h + 1))
                    src = ps[:, 2 + h % 2, :].rearrange("p (t v) -> p t v", v=HD)
                    if need_ctx:
                        a.activation(o_ret[:, 0:CT, h * HD:(h + 1) * HD], src[:, 4:6, :], ACT.Copy, scale=0.125)
                    a.activation(o_ret[:, CT:NT, h * HD:(h + 1) * HD], src[:, 0:4, :], ACT.Copy, scale=0.125).then_inc(sem("o_ret_ready"), 1)

                strips(0)
                strips(1)
                for h in range(4):
                    head_out(h)
                    if h + 2 < 4:
                        strips(h + 2)

            def fourier(l):
                need_ctx = l < DEPTH - 1
                tiles = tiles_of(l)
                need(act, "ret_scores", l, len(ret_items(l)))
                if need_ctx:
                    act.dma_start(dft_ctx[:, :, :, :], tab["dft_ctx"]).then_inc(sem("four_in"), 16)
                act.dma_start(chan[:, :, :], tab["chan"]).then_inc(sem("four_in"), 16)
                need(act, "mix_zero", l, 1)
                for g in range(4):
                    r = slice((g % 2) * HD, (g % 2) * HD + HD)
                    act.dma_start(mix_bd[r, g // 2, r], f_mix[l, g]).then_inc(sem("four_in"), 16)
                act.dma_start(gn_w[:, :], r_gn_w[l].partition_broadcast(P)).then_inc(sem("gn_in"), 16)
                need(act, "g_done", l, 1)
                a.activation(g_mat[:, :, :], ps[:, 4, :].rearrange("p (c n) -> p c n", c=2), ACT.Copy).then_inc(sem("g_ready"), 1)
                need(act, "ret_values", l, len(ret_items(l)))

                def group_sd(n):
                    need(act, "gvar", l, n + 1)
                    a.activation(gsd[:, n % 2, :], gmv[:, n % 2, :, 1], ACT.Sqrt, bias=eps[:, :]).then_inc(sem("gsd"), 1)

                group_sd(0)
                group_sd(1)
                for n, t in enumerate(tiles):
                    need(act, "ab_done", l, n + 1)
                    a.activation(four_ab[:, t, :], ps[:, 4 + (n + 1) % 2, :], ACT.Copy).then_inc(sem("ab_ready"), 1)
                for ch in range(2):
                    need(act, "four_done", l, ch + 1)
                    a.activation(act_hi[:, 4 + ch, CTX:TOK], ps[:, 6 + ch, :], ACT.Copy).then_inc(sem("four_hi"), 1)
                if need_ctx:
                    for ch in range(2):
                        need(act, "four_done", l, 2 + ch + 1)
                        a.activation(act_hi[:, 4 + ch, 0:CTX], ps[:, ch, 0:CTX], ACT.Copy).then_inc(sem("four_hi"), 1)
                for n, t in enumerate(tiles):
                    need(act, "y_T", l, n + 1)
                    a.activation(act_hi[:, 6:8, t * P:(t + 1) * P], ps[:, 4 + n % 2, 0:256].rearrange("p (k t) -> p k t", t=P),
                                 ACT.Copy).then_inc(sem("y_hi"), 1)
                    if n + 2 < len(tiles):
                        group_sd(n + 2)

            def load_norm(l, w, b):
                act.dma_start(bc[:, 2, :], w[l].partition_broadcast(P)).then_inc(sem("norm_in"), 16)
                act.dma_start(bc[:, 3, :], b[l].partition_broadcast(P)).then_inc(sem("norm_in"), 16)

            def gate_half(l, fh):
                width, parts = (384, 2) if l < DEPTH - 1 else (512, 1)
                lo_col = 0 if l < DEPTH - 1 else CTX
                g0 = SLOT0[(l, f"gu{fh}")]

                def chunk(e, done, free):
                    act.wait_ge(ring_used, done)
                    if free is not None:
                        need(act, "hid_ready", l, free)
                    ins = a.activation(silu_g[:, e, lo_col:TOK].rearrange("p (r n) -> p r n", r=parts),
                                       ps[:, 4 * e:4 * e + parts, 0:width], ACT.Silu)
                    ins.then_inc(sem("silu_ready"), 1)

                for e in range(2):
                    chunk(e, g0 + 4 * e + 4, None)
                with act.Fori(1, HALF // 2) as i:
                    for e in range(2):
                        chunk(e, i * 8 + (g0 + 4 * e + 4), i * 2 + (fh * HALF + e - 1))
                chunk(0, g0 + 4 * HALF, fh * HALF + HALF - 2)

            def down_hi(l, fh):
                cols = slice(0 if l < DEPTH - 1 else CTX, TOK)
                need(act, "hid_ready", l, (fh + 1) * HALF)
                for p in (2 * fh, 2 * fh + 1):
                    for j in range(HALF):
                        hid_slot_wait(act, l, p, j)
                        a.activation(hid_slot(p, j)[0][:, cols], hid[:, j, cols], ACT.Copy).then_inc(sem("hid_hi"), 1)

            act.dma_start(c_row[0:KC, :], c[0].rearrange("(k p) -> k p", p=P)).then_inc(c_in, 16)
            act.dma_start(c_row[KC:2 * KC, :], c_ctx.rearrange("(k p) -> k p", p=P)).then_inc(c_in, 16)
            act.dma_start(sel[:, :], tab["sel"]).then_inc(const_in, 16)
            act.dma_start(ident[:, :], tab["ident"]).then_inc(const_in, 16)
            act.dma_start(rope_seq[:, :, :, :], tab["rope_seq"]).then_inc(const_in, 16)
            act.dma_start(mask[:, :, :], tab["mask"]).then_inc(const_in, 16)
            act.dma_start(rope_grid[:, :, :, :], tab["rope_grid"]).then_inc(const_in, 16)
            act.dma_start(X[:, CT:NT, :], x[0].rearrange("(t p) d -> p t d", p=P)).then_inc(x_in, 16)
            act.dma_start(X[:, 0:CT, :], ctx_in[0].rearrange("(t p) d -> p t d", p=P)).then_inc(x_in, 16)
            act.wait_ge(c_in, 32)
            a.activation(c_row[:, :], c_row[:, :], ACT.Silu).then_inc(sem("c_row_ready"), 1)
            act.wait_ge(sem("c_T"), 1)
            a.activation(c_silu[:, :, :], ps[:, 0, 0:2 * KC].rearrange("p (s k) -> p s k", s=2), ACT.Copy).then_inc(c_ready, 1)
            mod_segment(0, "modA")
            act.wait_ge(x_in, 32)
            act.wait_ge(sem("eps_ready"), 1)
            norm_steps(("pre", 0), ALL, False)
            for l in range(DEPTH):
                tiles = tiles_of(l)
                nt = len(tiles)
                act.dma_start(qk_w[:, 0, :], a_q_norm[l].partition_broadcast(P)).then_inc(sem("qkw_in"), 16)
                act.dma_start(qk_w[:, 1, :], a_k_norm[l].partition_broadcast(P)).then_inc(sem("qkw_in"), 16)
                if l > 0:
                    act.dma_start(rope_grid[:, :, :, :], tab["rope_grid"]).then_inc(sem("qkw_in"), 16)
                    act.dma_start(rope_seq[:, :, :, :], tab["rope_seq"]).then_inc(sem("qkw_in"), 16)
                act.dma_start(sink[:, :], b_sink[l].partition_broadcast(P)).then_inc(sem("sink_in"), 16)
                act.dma_start(lg_raw[:, :], r_decay[l].rearrange("a b -> (a b)").partition_broadcast(P)).then_inc(sem("lg_in"), 16)
                project(l)
                mod_segment(l, "modB")
                need(act, "sink_in", l, 16)
                need(act, "post_ready", l, pre_count(l, 3, NT - 1))
                attention(l)
                need(act, "values_done", l, len(attn_items(l)))
                need(act, "o_T", l, 2 * nt)
                act.dma_start(delta[:, :], tab["delta"]).then_inc(sem("delta_in"), 16)
                act.dma_start(dft_lat[:, :, :, :], tab["dft_lat"]).then_inc(sem("four_in"), 16)
                retention(l)
                fourier(l)
                need(act, "four_done", l, 4 if l < DEPTH - 1 else 2)
                load_norm(l, ln1_w, ln1_b)
                mod_segment(l, "modG")
                norm_steps((l, 1), tiles, True)
                load_norm(l, ln2_w, ln2_b)
                gate_half(l, 0)
                mod_segment(l, "modC")
                down_hi(l, 0)
                gate_half(l, 1)
                if l < DEPTH - 1:
                    mod_segment(l + 1, "modA")
                down_hi(l, 1)
                norm_steps((l, 2), tiles, True)

        @block.vector
        def _(dve):
            v = nc.vector
            step_no = [0]

            def link(ins):
                step_no[0] += 1
                ins.then_inc(sem("dve_step"), 1)
                dve.wait_ge(sem("dve_step"), step_no[0])

            raised = {}

            def done(ins, name):
                raised[name] = raised.get(name, 0) + 1
                ins.then_inc(sem(name), 1)
                dve.wait_ge(sem(name), raised[name])

            def low(dst, src, high):
                return v.tensor_tensor(dst, src, high.bitcast(F32), ALU.subtract)

            def residual(l, seg, p, n, t, nt, last_slot, half, fresh):
                acc_wait(dve, l, seg, p, n, nt, last_slot)
                y = ps[:, t, :]
                cols = slice(half * 512, half * 512 + 512)
                link(v.tensor_tensor(y, y, bc[:, 0 if t >= CT else 1, cols], ALU.mult))
                if fresh:
                    ins = v.scalar_tensor_tensor(X[:, t, cols], X[:, t, cols], ALPHA, y, ALU.mult, ALU.add)
                else:
                    ins = v.tensor_tensor(X[:, t, cols], X[:, t, cols], y, ALU.add)
                done(ins, seg + "_read")

            def stats(t, o, signal):
                for h in range(2):
                    ins = v.bn_stats(st[:, t, o + 6 * h:o + 6 * h + 6], X[:, t, h * 512:(h + 1) * 512])
                link(ins)
                done(v.bn_aggr(st[:, t, o + 12:o + 14], st[:, t, o:o + 12]), signal)

            def scales(t, o, signal):
                link(v.reciprocal(st[:, t, o + 15:o + 16], st[:, t, o + 14:o + 15]))
                done(v.scalar_tensor_tensor(st[:, t, o + 16:o + 17], st[:, t, o + 12:o + 13], -1.0, st[:, t, o + 15:o + 16],
                                       ALU.mult, ALU.mult), signal)

            def norm_steps(key, tiles, post_norm, first):
                last = key == (DEPTH - 1, 2)
                nt = len(tiles)
                which = 0 if key[1] != 1 else 1
                if not last:
                    seg = "modB" if which else "modA"
                    lay = 0 if key[0] == "pre" else (key[0] if which else key[0] + 1)
                    dve.wait_ge(mod_out_read, mod_done(lay, seg))
                    link(v.tensor_scalar_add(mod_col[:, 2 * which + 1, :, :], mod_col[:, 2 * which + 1, :, :], 1.0))
                for step in range(nt + 6):
                    for s in (5, 4, 3, 2, 1, 0):
                        n = step - s
                        if not 0 <= n < nt:
                            continue
                        t = tiles[n]
                        stream = 0 if t >= CT else 1
                        if s == 0 and post_norm:
                            first(n, t)
                            stats(t, 0, "var1")
                        elif s == 1 and post_norm:
                            need(dve, "sd1", key, n + 1)
                            scales(t, 0, "scale1")
                        elif s == 2:
                            if post_norm:
                                if n == 0:
                                    need(dve, "norm_in", key[0], 32 * key[1])
                                need(dve, "normed", key, n + 1)
                                link(v.tensor_tensor(X[:, t, :], X[:, t, :], bc[:, 2, :], ALU.mult))
                                ins = v.tensor_tensor(X[:, t, :], X[:, t, :], bc[:, 3, :], ALU.add)
                                if last:
                                    done(ins, "x_ready")
                                else:
                                    link(ins)
                            if not last:
                                stats(t, 17, "var2")
                        elif s == 3 and not last:
                            need(dve, "sd2", key, n + 1)
                            scales(t, 17, "scale2")
                        elif s == 4 and not last:
                            need(dve, "xn_T", key, n + 1)
                            for k in range(KC):
                                ins = v.tensor_scalar(hbuf[:, n % 2, k * P:(k + 1) * P], ps[:, 6 + k // 4, (k % 4) * P:(k % 4 + 1) * P],
                                                      mod_col[:, 2 * which + 1, k, stream:stream + 1],
                                                      mod_col[:, 2 * which, k, stream:stream + 1], ALU.mult, ALU.add)
                            done(ins, "h_ready")
                        elif s == 5 and not last:
                            need(dve, "h_hi", key, n + 1)
                            c = slice(t * P, (t + 1) * P)
                            done(low(act_lo[:, :, c], hbuf[:, n % 2, :].rearrange("p (k t) -> p k t", k=KC),
                                act_hi[:, :, c]), "act_ready")

            def project(l):
                tp = [0]

                def by_head(q):
                    return q[:, 0:256].rearrange("p (a b d) -> p a b d", a=2, b=2)

                def by_key_head(q):
                    return q[:, 0:256].rearrange("p (b a d) -> p a b d", a=2, b=2)

                def rotate(dst, src, heads, grid, t):
                    table = (rope_grid if grid else rope_seq)[:, t - CT, :, :]
                    s3 = src.rearrange("p (h d) -> p h d", d=HD)
                    axes, part = (2, 16) if grid else (1, 32)
                    n = heads * HD
                    pat = "p (h a s d) -> p h a s d"
                    sw = dict(a=axes, s=2, d=part)
                    t5 = tmp2[:, 0:n].rearrange(pat, **sw)
                    s5 = src.rearrange(pat, **sw)
                    sin = table[:, 1, :].rearrange("p (a s d) -> p a s d", **sw)
                    for s in range(2):
                        ins = v.tensor_tensor(t5[:, :, :, s, :], s5[:, :, :, 1 - s, :],
                                              sin[:, :, s, :].unsqueeze(1).to_broadcast([P, heads, axes, part]), ALU.mult)
                    link(ins)
                    link(v.tensor_tensor(s3, s3, table[:, 0, :].unsqueeze(1).to_broadcast([P, heads, HD]), ALU.mult))
                    if heads == 6:
                        v.tensor_tensor(by_key_head(dst), by_head(src), by_head(tmp2), ALU.add)
                        return v.tensor_tensor(dst[:, 256:384], src[:, 256:384], tmp2[:, 256:384], ALU.add)
                    return v.tensor_tensor(dst, src, tmp2[:, 0:n], ALU.add)

                def arrange(b, n, t):
                    lat = t >= CT
                    o = post[:, tp[0] % 2, :]
                    if tp[0] >= 2:
                        need(dve, "qk_T", l, tp[0] - 1)
                    src = pre[:, t, :]
                    if b == 0:
                        need(dve, "rms_sd", l, n + 1)
                        link(v.reciprocal(ssq[:, t, :], rms[:, t, :]))
                        link(v.tensor_tensor(tmp1[:, 0:384].rearrange("p (h d) -> p h d", d=HD),
                                             src[:, 0:384].rearrange("p (h d) -> p h d", d=HD),
                                             ssq[:, t, :].unsqueeze(2).to_broadcast([P, 6, HD]), ALU.mult))
                        dst, q_to = (tmp1, by_head) if lat else (o, by_key_head)
                        v.tensor_tensor(q_to(dst), by_head(tmp1),
                                        qk_w[:, 0:1, :].unsqueeze(1).to_broadcast([P, 2, 2, HD]), ALU.mult)
                        ins = v.tensor_tensor(dst[:, 256:384].rearrange("p (h d) -> p h d", d=HD),
                                              tmp1[:, 256:384].rearrange("p (h d) -> p h d", d=HD),
                                              qk_w[:, 1:2, :].to_broadcast([P, 2, HD]), ALU.mult)
                        if lat:
                            link(ins)
                            ins = rotate(o[:, 0:384], tmp1[:, 0:384], 6, True, t)
                    elif b == 1:
                        if lat:
                            ins = rotate(o[:, 0:384], src[:, 0:384], 6, True, t)
                        else:
                            v.tensor_copy(by_key_head(o), by_head(src))
                            ins = v.tensor_copy(o[:, 256:384], src[:, 256:384])
                    elif b == 2:
                        if lat:
                            v.tensor_copy(o[:, 0:256], src[:, 0:256])
                            ins = rotate(o[:, 256:512], src[:, 256:512], 4, False, t)
                        else:
                            ins = v.tensor_copy(o, src)
                    else:
                        ins = rotate(o[:, 0:256], src[:, 0:256], 4, False, t) if lat else v.tensor_copy(o[:, 0:256], src[:, 0:256])
                    done(ins, "post_ready")
                    tp[0] += 1

                need(dve, "qkw_in", l, 32 if l == 0 else 64)
                for b in range(4):
                    tiles = block_tiles(l, b)
                    if b == 0:
                        for n, t in enumerate(tiles):
                            need(dve, "pre_ready", l, n + 1)
                            link(v.tensor_tensor(tmp2[:, 0:384], pre[:, t, 0:384], pre[:, t, 0:384], ALU.mult))
                            done(v.reduce_sum(ssq[:, t, :], tmp2[:, 0:384].rearrange("p (h d) -> p h d", d=HD), AX), "ssq_ready")
                    for n, t in enumerate(tiles):
                        need(dve, "pre_ready", l, pre_count(l, b, n))
                        arrange(b, n, t)

            def attention(l):
                items = attn_items(l)
                total = len(items)

                def maxima(i):
                    g, t, h, keys = items[i]
                    need(dve, "scores_ready", l, i + 1)
                    flat = ps[:, 2 * (i % 2):2 * (i % 2) + 2, :].rearrange("p b n -> p (b n)")
                    m = slice(i % 4, i % 4 + 1)
                    link(v.reduce_max(rowmax[:, m], flat[:, 0:len(keys) * P], AX))
                    if g == "A":
                        ins = v.tensor_scalar_mul(negmax[:, m], rowmax[:, m], -0.125)
                    else:
                        ins = v.tensor_scalar(negmax[:, m], rowmax[:, m], -0.125, nsink[:, h:h + 1], ALU.mult, ALU.min)
                    done(ins, "neg_ready")

                def read_T(i):
                    g, t, h, keys = items[i]
                    need(dve, "probs_T_done", l, i + 1)
                    if i >= 2:
                        need(dve, "values_done", l, i - 1)
                    n = min(len(keys), 4) * P
                    done(v.tensor_copy(probs_T[:, i % 2, 0:n], ps[:, 4, 0:n]), "probs_T_ready")

                def output(i):
                    g, t, h, keys = items[i]
                    m = slice(i % 4, i % 4 + 1)
                    q = i // 4
                    if g == "B":
                        link(v.tensor_tensor(expsum[:, m], expsum[:, m], expsink[:, m], ALU.add))
                    link(v.reciprocal(rden[:, m], expsum[:, m]))
                    need(dve, "values_done", l, i + 1)
                    if q >= 2 and h == 0:
                        need(dve, "o_T", l, q - 1)
                    done(v.tensor_scalar_mul(o_attn[:, q % 2, h * HD:(h + 1) * HD], ps[:, 6 + i % 2, 0:HD],
                                        rden[:, m]), "o_read")

                def out_low(q):
                    g, t, _, _ = items[4 * q]
                    need(dve, "o_hi", l, q + 1)
                    ch = 0 if g == "A" else 2
                    c = slice(t * P, (t + 1) * P)
                    done(low(act_lo[:, ch:ch + 2, c], ps[:, 7, 256:512].rearrange("p (k t) -> p k t", t=P),
                        act_hi[:, ch:ch + 2, c]), "o_T_lo")

                need(dve, "sink_in", l, 16)
                link(v.tensor_scalar_mul(nsink[:, :], sink[:, :], -1.0))
                for s in range(total + 5):
                    if s < total:
                        maxima(s)
                    if 2 <= s < total + 2:
                        read_T(s - 2)
                    if 3 <= s < total + 3:
                        need(dve, "probs_ready", l, s - 2)
                        output(s - 3)
                    if s >= 4 and (s - 4) % 4 == 3 and s - 4 < total:
                        out_low((s - 4) // 4)

            def retention(l):
                items = ret_items(l)
                per = len(items) // 4

                def strip_arg(h):
                    link(v.tensor_scalar_mul(strip[:, h % 2, :], delta[:, 0:896], lg[:, 0, h:h + 1]))
                    done(v.scalar_tensor_tensor(strip[:, h % 2, :], delta[:, 0:896], lg[:, 1, h:h + 1], strip[:, h % 2, :],
                                           ALU.mult, ALU.min), "strip_arg")

                def strip_end(h):
                    need(dve, "strip_exp", l, 3 * (h + 1))
                    v.tensor_tensor(strip[:, h % 2, 384:512], strip[:, h % 2, 384:512], ident[:, :], ALU.add)
                    done(v.tensor_tensor(strip_ctx[:, h % 2, :], strip_ctx[:, h % 2, :], ctx_part[:, :], ALU.add), "strip_ready")

                def decays(h):
                    need(dve, "strip_ready", l, h + 1)
                    for i in range(per * h, per * (h + 1)):
                        _, s, lat = items[i]
                        need(dve, "ret_scores", l, i + 1)
                        if i >= 2:
                            need(dve, "ret_values", l, i - 1)
                        n = SEQ if lat else CTX
                        if lat and s < CT:
                            d = strip_ctx[:, h % 2, P - P * s:P - P * s + n]
                        else:
                            k = s - CT if lat else s
                            d = strip[:, h % 2, 384 - P * k:384 - P * k + n]
                        done(v.tensor_tensor(decayed[:, i % 2, 0:n], ps[:, i % 2, 0:n], d, ALU.mult), "decayed_ready")

                need(dve, "lg_ln", l, 1)
                v.tensor_scalar_mul(lg[:, 0, :], lg_raw[:, 0:4], -1.0)
                v.tensor_copy(lg[:, 1, :], lg_raw[:, 4:8])
                link(v.tensor_scalar_mul(lg[:, 2, :], lg_raw[:, 4:8], -float(SEQ + P)))
                need(dve, "delta_in", l, 16)
                strip_arg(0)
                strip_arg(1)
                strip_end(0)
                strip_end(1)
                decays(0)
                strip_arg(2)
                decays(1)
                strip_end(2)
                strip_arg(3)
                decays(2)
                strip_end(3)
                decays(3)

            def fourier(l):
                need_ctx = l < DEPTH - 1
                tiles = tiles_of(l)

                def group_norm(n):
                    t = tiles[n]
                    e = n % 2
                    v.tensor_tensor(gate_ret[:, t, :], gate_ret[:, t, :], gn_w[:, :], ALU.mult)
                    for h in range(4):
                        ins = v.bn_stats(gst[:, e, h, :], o_ret[:, t, h * HD:(h + 1) * HD])
                    link(ins)
                    for h in range(4):
                        ins = v.bn_aggr(gmv[:, e, h, :], gst[:, e, h, :])
                    done(ins, "gvar")
                    need(dve, "gsd", l, n + 1)
                    link(v.reciprocal(grs[:, e, :], gsd[:, e, :]))
                    if n >= 2:
                        need(dve, "y_T", l, n - 1)
                    for h in range(4):
                        c = slice(h * HD, (h + 1) * HD)
                        ins = v.tensor_scalar(y_ret[:, e, c], o_ret[:, t, c], gmv[:, e, h, 0:1], grs[:, e, h:h + 1],
                                              ALU.subtract, ALU.mult)
                    link(ins)
                    done(v.tensor_tensor(y_ret[:, e, :], y_ret[:, e, :], gate_ret[:, t, :], ALU.mult), "y_ret_ready")

                done(v.memset(mix_bd[:, :, :], 0.0), "mix_zero")
                need(dve, "gn_in", l, 16)
                need(dve, "o_ret_ready", l, 4)
                group_norm(0)
                group_norm(1)
                for n in range(4 if need_ctx else 2):
                    need(dve, "four_hi", l, n + 1)
                    ch = n % 2
                    src, c = (ps[:, 6 + ch, :], slice(CTX, TOK)) if n < 2 else (ps[:, ch, 0:CTX], slice(0, CTX))
                    done(low(act_lo[:, 4 + ch, c], src, act_hi[:, 4 + ch, c]), "four_lo")
                for n, t in enumerate(tiles):
                    need(dve, "y_hi", l, n + 1)
                    c = slice(t * P, (t + 1) * P)
                    done(low(act_lo[:, 6:8, c], ps[:, 4 + n % 2, 0:256].rearrange("p (k t) -> p k t", t=P),
                        act_hi[:, 6:8, c]), "y_lo")
                    if n + 2 < len(tiles):
                        group_norm(n + 2)

            def up_half(l, fh):
                width, parts = (384, 2) if l < DEPTH - 1 else (512, 1)
                lo_col = 0 if l < DEPTH - 1 else CTX

                def chunk(e, j, ready):
                    need(dve, "silu_ready", l, ready)
                    pat = dict(r=parts)
                    done(v.tensor_tensor(hid[:, j, lo_col:TOK].rearrange("p (r n) -> p r n", **pat),
                                    silu_g[:, e, lo_col:TOK].rearrange("p (r n) -> p r n", **pat),
                                    ps[:, 4 * e + 2:4 * e + 2 + parts, 0:width], ALU.mult), "hid_ready")

                for f in range(HALF):
                    chunk(f % 2, f, fh * HALF + f + 1)

            def down_low(l, fh):
                tiles = tiles_of(l)
                nt = len(tiles)
                cols = slice(0 if l < DEPTH - 1 else CTX, TOK)

                def lows(p, js):
                    for j in js:
                        hi_, lo_ = hid_slot(p, j)
                        need(dve, "hid_hi", l, p * HALF + j + 1)
                        done(low(lo_[:, cols], hid[:, j, cols], hi_[:, cols]), "hid_split")

                p = 2 * fh
                lows(p, range(HALF))
                lows(p + 1, range(2))
                for n, t in enumerate(tiles):
                    residual(l, "dn", p, n, t, nt, dn_slot(l, p, HALF - 1), 0, fh == 0)
                lows(p + 1, range(2, HALF))
                if fh == 0:
                    for n, t in enumerate(tiles):
                        residual(l, "dn", p + 1, n, t, nt, dn_slot(l, p + 1, HALF - 1), 1, True)

            done(v.memset(eps[:, :], EPS), "eps_ready")
            dve.wait_ge(x_in, 32)
            dve.wait_ge(const_in, 16 * N_CONST)
            norm_steps(("pre", 0), ALL, False, None)
            for l in range(DEPTH):
                tiles = tiles_of(l)
                nt = len(tiles)
                project(l)
                attention(l)
                retention(l)
                fourier(l)
                dve.wait_ge(mod_out_read, mod_done(l, "modG"))
                last = SLOT0[(l, "wout")] + 7
                for n, t in enumerate(tiles):
                    residual(l, "wout", 0, n, t, nt, last, 0, True)

                def first_1(n, t):
                    residual(l, "wout", 1, n, t, nt, last + 8, 1, True)
                    need(dve, "wout_read", l, nt + n + 1)

                def first_2(n, t):
                    residual(l, "dn", 3, n, t, nt, dn_slot(l, 3, HALF - 1), 1, False)
                    need(dve, "dn_read", l, 3 * nt + n + 1)

                norm_steps((l, 1), tiles, True, first_1)
                up_half(l, 0)
                dve.wait_ge(mod_out_read, mod_done(l, "modC"))
                down_low(l, 0)
                up_half(l, 1)
                down_low(l, 1)
                norm_steps((l, 2), tiles, True, first_2)


_INS = ["x", "c", "ctx", "c_ctx", "w_mod", "b_mod", "w_in", "a_q_norm", "a_k_norm", "b_sink", "f_mix", "r_decay",
        "r_gn_w", "w_out", "ln1_w", "ln1_b", "w_gate_up", "w_down", "ln2_w", "ln2_b"]
_OUTS = [((1, SEQ, D), "float32")]


def kernel(**inputs):
    import numpy as _np
    import concourse.bacc as _bacc
    from concourse import mybir as _mybir
    from concourse.bass_utils import run_bass_kernel_spmd as _run

    nc = _bacc.Bacc("TRN2", target_bir_lowering=False, num_devices=1)
    arrays, args = {}, []
    for name in _INS:
        a = _np.ascontiguousarray(inputs[name])
        arrays[f"in_{name}_dram"] = a
        args.append(nc.dram_tensor(f"in_{name}_dram", a.shape, _mybir.dt.from_np(a.dtype), kind="ExternalInput").ap())
    for i, (shape, dtype) in enumerate(_OUTS):
        dt = _mybir.dt.from_np(_np.dtype(dtype))
        args.append(nc.dram_tensor(f"out_{i}_dram", shape, dt, kind="ExternalOutput").ap())
    build(nc, *args)
    r = _run(nc, [arrays], core_ids=[0])
    got = tuple(r.results[0][f"out_{i}_dram"] for i in range(len(_OUTS)))
    return got[0]
```

```python
from contextlib import ExitStack

import numpy as np
import concourse.bass as bass
from concourse import mybir

ALU = mybir.AluOpType
ACT = mybir.ActivationFunctionType
F32 = mybir.dt.float32
R32 = mybir.dt.float32r
AX = mybir.AxisListType.X

P = 128
D = 1024
DEPTH = 2
CTX, SEQ = 256, 512
TOK = CTX + SEQ
NT = TOK // P
CT = CTX // P
HD = 64
FF = 2816
FC = FF // P
HALF = FC // 2
KC = D // P
GRID_W = 64
ALPHA = (2.0 * DEPTH) ** 0.25
EPS = 1e-6
NEG = -1e30
RING = 8
LAT = list(range(CT, NT))
ALL = list(range(NT))

SEGMENTS = {"modA": [0] * 8, "win": [4] * 9, "modB": [0] * 8, "modG": [0] * 4, "wout": [4] * 4, "modC": [0] * 4,
            "gu0": [4] * HALF, "dn0": [4, 4, 3] * 2, "gu1": [4] * HALF, "dn1": [4, 4, 3] * 2}
MOD_BLOCKS = {"modA": [0, 1, 2, 3], "modB": [6, 7, 8, 9], "modG": [4, 5], "modC": [10, 11]}


def plan():
    order = [(0, "modA")]
    for l in range(DEPTH):
        order += [(l, "win"), (l, "modB")]
        if l + 1 < DEPTH:
            order.append((l + 1, "modA"))
        order += [(l, s) for s in ("modG", "wout", "gu0", "modC", "dn0", "gu1", "dn1")]
    unit0, slot0, block0, units = {}, {}, {}, []
    slots = mods = blocks = 0
    sent = [0, 0]
    for key in order:
        unit0[key], slot0[key], block0[key] = len(units), slots, blocks
        for n in SEGMENTS[key[1]]:
            slots += n
            mods += n == 0 and key == (0, "modA")
            sent[len(units) % 2] += 2 if key[1][:2] == "gu" else 1
            units.append((key, n, slots, mods, sent[len(units) % 2]))
        blocks += len(MOD_BLOCKS.get(key[1], ()))
    return order, unit0, slot0, block0, units


ORDER, UNIT0, SLOT0, BLOCK0, UNITS = plan()


def tables():
    f = np.float32
    t = {"ident": np.eye(P, dtype=f)}

    def rot(pos, n):
        inv = (f(10000.0) ** (-np.arange(n, dtype=f) / f(n))).astype(f)
        ang = (pos.astype(f)[:, None] * inv[None, :]).astype(f).astype(np.float64)
        return np.cos(ang), np.sin(ang)

    pos = np.arange(SEQ)
    cr, sr = rot(pos // GRID_W, 16)
    cc, sc = rot(pos % GRID_W, 16)
    cs, ss = rot(pos, 32)
    grid = np.stack([np.concatenate([cr, cr, cc, cc], 1), np.concatenate([-sr, sr, -sc, sc], 1)], 1)
    seq = np.stack([np.concatenate([cs, cs], 1), np.concatenate([-ss, ss], 1)], 1)
    for name, a in (("rope_grid", grid), ("rope_seq", seq)):
        t[name] = a.reshape(SEQ // P, P, 2, HD).transpose(1, 0, 2, 3).astype(f)
    q, j = np.arange(P)[:, None], np.arange(P)[None, :]
    t["mask"] = np.stack([np.where(j >= q, 0, NEG), np.where(j <= q, 0, NEG)], 1).astype(f)
    t["delta"] = (np.arange(-384, 768)[None, :] - q).astype(f)
    a = 2 * np.pi * (np.outer(np.arange(HD), np.arange(HD)) % HD) / HD
    ch = np.zeros((P, 2, P))
    for g in range(2):
        s = slice(g * HD, g * HD + HD)
        ch[s, 0, s] = np.cos(a) / np.sqrt(HD)
        ch[s, 1, s] = -np.sin(a) / np.sqrt(HD)
    t["chan"] = ch.astype(f)
    for name, n in (("dft_lat", SEQ), ("dft_ctx", CTX)):
        a = 2 * np.pi * (np.outer(np.arange(n), np.arange(n)) % n) / n
        m = np.stack([np.cos(a), np.sin(a)], 1) / np.sqrt(n)
        t[name] = m.reshape(n // P, P, 2, n).transpose(1, 0, 2, 3).astype(f)
    t["sel"] = np.array([[1, 0], [0, 1], [1, 1]], f)
    return {k: np.ascontiguousarray(v) for k, v in t.items()}


def build(nc, x, c, ctx_in, c_ctx, w_mod, b_mod, w_in, a_q_norm, a_k_norm, b_sink, f_mix, r_decay,
          r_gn_w, w_out, ln1_w, ln1_b, w_gate_up, w_down, ln2_w, ln2_b, out):
    tab = {k: nc.inline_tensor(v, name="tab_" + k)[tuple(slice(None) for _ in v.shape)] for k, v in tables().items()}
    stack = ExitStack()
    with stack:
        base = (nc.sbuf_base + 63) // 64 * 64
        at = [base]

        def place(name, shape, dt=F32, offset=None):
            size = int(np.prod(shape[1:])) * 4
            if offset is None:
                offset = at[0]
                at[0] += (size + 31) // 32 * 32
            return nc.alloc_sbuf_tensor_at(name, shape, dt, offset=offset)

        X = place("resid", [P, NT, D])
        act_hi = place("act_hi", [P, KC, TOK], R32)
        q_pad_ret = place("q_pad_ret", [P, 2, TOK], offset=at[0] - 4 * TOK * 4)
        HI_END = at[0]
        act_lo = place("act_lo", [P, KC, TOK], R32)
        LO_END = at[0]
        mod_acc = place("mod_acc", [P, 2, 2, 512], offset=at[0] - 4 * TOK * 4)
        mod_tmp = place("mod_tmp", [P, 512], offset=at[0] - 4 * TOK * 4 + 8192)
        stage = place("stage", [P, 2, 2048])
        ring_hi = place("ring_hi", [P, RING, 512], R32)
        ring_lo = place("ring_lo", [P, RING, 512], R32)
        PR = at[0]
        at[0] += 62720
        BR = at[0]
        at[0] += 16384
        qk_attn = {"A": place("qk_A", [P, 3, TOK], offset=PR), "B": place("qk_B", [P, 3, TOK], offset=PR + 12288)}
        v_attn = {"A": place("v_A", [P, NT, P], offset=PR + 9216), "B": place("v_B", [P, NT, P], offset=PR + 21504)}
        q_ret = place("q_ret", [P, 2, TOK], offset=PR + 24576)
        k_ret = place("k_ret", [P, 2, TOK], offset=PR + 30720)
        v_ret = place("v_ret", [P, NT, 256], offset=PR + 36864)
        gate_ret = place("gate_ret", [P, NT, 256], offset=PR + 43008)
        u_four = place("u_four", [P, 2, TOK], offset=PR + 49152)
        post = place("post", [P, 2, 512], offset=PR + 55296)
        rope_grid = place("rope_grid", [P, 4, 2, HD], offset=PR + 60160)
        pre = place("pre", [P, NT, 512], offset=BR)
        tmp1 = place("tmp1", [P, 512], offset=BR + 12288)
        tmp2 = place("tmp2", [P, 512], offset=BR + 14336)
        probs = place("probs", [P, 3, TOK], offset=BR)
        probs_T = place("probs_T", [P, 2, TOK], offset=BR + 9216)
        o_attn = place("o_attn", [P, 2, 256], offset=PR + 60160)
        delta = place("delta", [P, 1152], offset=PR + 55296)
        ctx_part = place("ctx_part", [P, 640], offset=PR + 60160)
        strip = place("strip", [P, 2, 896], offset=BR)
        strip_ctx = place("strip_ctx", [P, 2, 640], offset=BR + 7168)
        decayed = place("decayed", [P, 2, 512], offset=BR + 12288)
        dft_lat = place("dft_lat", [P, 4, 2, 512], offset=PR)
        o_ret = place("o_ret", [P, NT, 256], offset=PR + 16384)
        g_mat = place("g_mat", [P, 2, 256], offset=PR + 22528)
        dft_ctx = place("dft_ctx", [P, 2, 2, 256], offset=HI_END - 2 * TOK * 4)
        chan = place("chan", [P, 2, P], offset=LO_END - 2048)
        mix_bd = place("mix_bd", [P, 2, P], offset=LO_END - 1024)
        gst = place("gst", [P, NT, 4, 6], offset=PR + 24576)
        gmv = place("gmv", [P, NT, 4, 2], offset=PR + 25152)
        gsd = place("gsd", [P, NT, 4], offset=PR + 25344)
        grs = place("grs", [P, NT, 4], offset=PR + 25440)
        gn_w = place("gn_w", [P, 256], offset=PR + 32768)
        four_ab = place("four_ab", [P, NT, 512], offset=BR)
        hid = place("hid", [P, HALF, TOK], offset=PR)
        silu_g = place("silu_g", [P, 2, TOK], offset=PR + 33792)
        hs_hi = place("hs_hi", [P, 3, TOK], R32, offset=PR + 39936)
        hs_lo = place("hs_lo", [P, 3, TOK], R32, offset=PR + 49152)
        xn = place("xn", [P, 2, D], offset=PR + 39936)
        hbuf = place("hbuf", [P, 2, D], offset=PR + 48128)
        bc = place("bc", [P, 4, D], offset=BR)
        mod_acc_ffn = place("mod_acc_ffn", [P, 2, 2, 512], offset=PR + 39936)
        mod_tmp_ffn = place("mod_tmp_ffn", [P, 512], offset=PR + 48128)
        ident = place("ident", [P, P])
        rope_seq = place("rope_seq", [P, 4, 2, HD])
        padded = place("padded", [P, 4, P], offset=at[0] - 2048)
        mask = place("mask", [P, 2, P])
        mod_row = place("mod_row", [3, 2, 512])
        qk_w = place("qk_w", [P, 2, HD])
        st = place("st", [P, NT, 34])
        c_row = place("c_row", [2 * KC, P], offset=PR)
        c_silu = place("c_silu", [P, 2, KC])
        mod_col = place("mod_col", [P, 4, KC, 2])
        ssq = place("ssq", [P, NT, 6])
        rms = place("rms", [P, NT, 6])
        sink = place("sink", [P, 4])
        nsink = place("nsink", [P, 4])
        lg_raw = place("lg_raw", [P, 8])
        lg = place("lg", [P, 3, 4])
        rowmax = place("rowmax", [P, 4])
        negmax = place("negmax", [P, 4])
        expsum = place("expsum", [P, 4])
        expsink = place("expsink", [P, 4])
        rden = place("rden", [P, 4])
        eps = place("eps", [P, 1])
        sel = place("sel", [3, 2])
        pick = place("pick", [P, 2, 2])
        assert at[0] <= nc.sbuf_usable_end, at[0]

        ps = stack.enter_context(nc.psum_tensor("ps", [P, 8, 512], F32))

        sems = {}

        def sem(*name):
            key = "_".join(str(n) for n in name)
            if key not in sems:
                sems[key] = stack.enter_context(nc.semaphore(key))
            return sems[key]

        x_in, c_in, const_in = sem("x_in"), sem("c_in"), sem("const_in")
        unit_in = [sem("unit_in", 0), sem("unit_in", 1)]
        bias_row_in = [sem("bias_row_in", 0), sem("bias_row_in", 1)]
        w_hi, w_ready, ring_used, mod_used = sem("w_hi"), sem("w_ready"), sem("ring_used"), sem("mod_used")
        mod_row_ready, mod_out, mod_out_read = sem("mod_row_ready"), sem("mod_out"), sem("mod_out_read")
        mod_partial, mod_summed = sem("mod_partial"), sem("mod_summed")
        mod_product, mod_added = sem("mod_product"), sem("mod_added")
        c_ready = sem("c_ready")
        N_CONST = 5

        def tiles_of(l):
            return ALL if l < DEPTH - 1 else LAT

        def block_tiles(l, b):
            return tiles_of(l) if b in (2, 4) else ALL

        def pre_count(l, b, n):
            return sum(len(block_tiles(l, a)) for a in range(b)) + n + 1

        def unit_wait(e, u):
            e.wait_ge(unit_in[u % 2], 16 * UNITS[u][4])

        def unit_release_wait(e, u):
            _, n, slots, mods, _ = UNITS[u]
            if n:
                e.wait_ge(w_ready, slots)
            else:
                (l, seg), i = UNITS[u][0], (u - UNIT0[UNITS[u][0]])
                if (l, seg, i // 2) in FILL_NO:
                    item, k = (l, seg, i // 2), 4 * (i % 2 + 1)
                    e.wait_ge(mod_partial, KC * FILL_NO[item] + k)
                    if not on_vector(item):
                        e.wait_ge(mod_product, KC * POOL_NO[item] + k)
                else:
                    e.wait_ge(mod_used, mods)

        MOD_KEYS = [(*key, i) for key in ORDER for i in range(len(MOD_BLOCKS.get(key[1], ())))]
        MOD_OUT = {}
        n_out = 0
        for key in ORDER:
            for i, _ in enumerate(MOD_BLOCKS.get(key[1], ())):
                k = 1 if key[1] in ("modA", "modB") else (2 if key[0] < DEPTH - 1 else 1)
                MOD_OUT[(*key, i)] = (n_out, k)
                n_out += k

        def mod_done(l, seg):
            n, k = MOD_OUT[(l, seg, len(MOD_BLOCKS[seg]) - 1)]
            return n + k

        def acc_wait(e, l, seg, p, n, nt, last_slot):
            if n == nt - 1:
                e.wait_ge(ring_used, last_slot + 1)
            else:
                need(e, seg + "_acc", l, p * (nt - 1) + n + 1)

        def win_last_slot(l, b):
            return SLOT0[(l, "win")] + (8 * b + 7 if b < 4 else 35)

        def dn_slot(l, p, j):
            return SLOT0[(l, f"dn{p // 2}")] + (p % 2) * HALF + j

        def hid_slot(p, j):
            if p < 2:
                s = (p * HALF + j) % 3
                return hs_hi[:, s, :], hs_lo[:, s, :]
            s = ((p - 2) * HALF + j) % 8
            return act_hi[:, s, :], act_lo[:, s, :]

        def hid_slot_wait(e, l, p, j):
            n, depth = (p % 2) * HALF + j, 3 if p < 2 else 8
            if n >= depth:
                m = n - depth
                e.wait_ge(ring_used, dn_slot(l, p - p % 2 + m // HALF, m % HALF) + 1)
            elif p >= 2:
                e.wait_ge(ring_used, SLOT0[(l, "dn1")])

        def attn_items(l):
            items = []
            for g in "AB":
                for t in tiles_of(l):
                    if t < CT:
                        keys = [0, 1]
                    elif g == "A":
                        keys = ALL
                    else:
                        keys = [0, 1] + [k for k in (t - 1, t, t + 1) if CT <= k < NT]
                    items += [(g, t, h, keys) for h in range(4)]
            return items

        def ret_items(l):
            items = []
            for h in range(4):
                items += [(h, s, True) for s in ALL]
                if l < DEPTH - 1:
                    items += [(h, s, False) for s in range(CT)]
            return items

        def attn_fill(l):
            return [(l, "modB", i) for i in range(4)] + [(l + 1, "modA", i) for i in range(2 if l + 1 < DEPTH else 0)]

        def ret_fill(l):
            return [(l + 1, "modA", i) for i in range(2, 4 if l + 1 < DEPTH else 2)] + [(l, "modG", i) for i in range(2)]

        def ffn_fill(l):
            return [(l, "modC", i) for i in range(2)]

        FILL_NO = {item: n for n, item in enumerate(i for l in range(DEPTH) 
                                                    for i in attn_fill(l) + ret_fill(l) + ffn_fill(l))}

        def on_vector(item):
            return item[1:] == ("modC", 1)

        POOL_NO = {item: n for n, item in enumerate(i for i in FILL_NO if not on_vector(i))}

        def partial_sums(item):
            acc, tmp = (mod_acc_ffn, mod_tmp_ffn) if item[1] == "modC" else (mod_acc, mod_tmp)
            return acc[:, (BLOCK0[item[:2]] + item[2]) % 2, :, :], tmp[:, :]

        def norm_tiles(key):
            return NT if key[0] == "pre" else len(tiles_of(key[0]))

        def wait_low(e, key, n):
            first = norm_tiles(key) - 2
            need(e, "act_ready", key, n + 1) if n < first else need(e, "last_ready", key, n - first + 1)

        def shared_modulation(key, n):
            return key[0] == "pre" or n >= len(tiles_of(key[0])) - 2

        NORMS = [("pre", 0)] + [(l, w) for l in range(DEPTH) for w in (1, 2)]

        def signals(name, l):
            if isinstance(l, tuple):
                if name == "scale_plus_1":
                    return 1
                if name in ("act_ready", "last_ready"):
                    return 0 if l == (DEPTH - 1, 2) else 2 if name[0] == "l" else (NT if l[0] == "pre" else len(tiles_of(l[0]))) - 2
                if name == "h_half":
                    return 0 if l == (DEPTH - 1, 2) else NT if l[0] == "pre" else 2
                if l[0] == "pre":
                    return 0 if name in ("var1", "sd1") else NT
                return len(tiles_of(l[0]))
            nt, blocks = len(tiles_of(l)), [len(block_tiles(l, b)) for b in range(5)]
            n_attn, n_ret, need_ctx = len(attn_items(l)), len(ret_items(l)), l < DEPTH - 1
            return {
                "win_acc": sum(blocks) - 5, "wout_acc": 2 * (nt - 1), "dn_acc": 4 * (nt - 1),
                "pre_ready": sum(blocks), "post_ready": sum(blocks[:4]), "qk_T": sum(blocks[:4]),
                "qk_read": sum(blocks[:4]), "ssq_ready": NT, "rms_sd": NT, "qkw_in": 32 if l == 0 else 64,
                "scores_ready": n_attn, "neg_ready": n_attn, "probs_ready": n_attn, "probs_T_done": n_attn,
                "probs_T_ready": n_attn, "probs_T2_ready": sum(len(i[3]) > 4 for i in attn_items(l)),
                "values_done": n_attn, "o_read": n_attn, "o_T": 2 * nt, "o_hi": 2 * nt, "o_T_lo": 2 * nt,
                "sink_in": 16, "lg_in": 16, "lg_exp": 1, "pad_zero": 1, "q_pad": n_attn, "ret_q_pad": 4, "lg_ln": 1, "lg_set": 1, "delta_in": 16,
                "ret_scores": n_ret, "decayed_ready": n_ret, "ret_values": n_ret, "o_ret_ready": 4,
                "strip_arg": 4, "strip_exp": 12, "strip_ready": 4,
                "four_in": 16 * (7 if need_ctx else 6), "gn_in": 16, "mix_zero": 1, "g_done": 1, "g_ready": 1,
                "ab_done": nt, "ab_ready": nt, "gvar": 1, "gsd": 1, "y_ret_ready": nt, "y_T": nt, "y_hi": nt,
                "y_lo": nt, "four_done": 4 if need_ctx else 2, "four_hi": 4 if need_ctx else 2,
                "four_lo": 4 if need_ctx else 2, "norm_in": 64, "silu_ready": 2 * HALF, "hid_ready": 2 * HALF,
                "hid_hi": 4 * HALF, "hid_split": 4 * HALF, "wout_read": 2 * nt, "dn_read": 4 * nt,
            }[name]

        def need(e, name, l, n):
            before = NORMS[:NORMS.index(l)] if isinstance(l, tuple) else range(l)
            e.wait_ge(sem(name), n + sum(signals(name, k) for k in before))

        block = stack.enter_context(nc.Block())

        @block.sync
        def _(sp):
            def send(u, src):
                if u >= 2:
                    unit_release_wait(sp, u - 2)
                sp.dma_start(stage[:, u % 2, 0:src[1]].rearrange(src[2], **src[3]), src[0]).then_inc(unit_in[u % 2], 16)

            def rows(w, k0, n, c0, width):
                return (w[k0 * P:(k0 + n) * P, c0:c0 + width].rearrange("(k p) c -> p k c", p=P), n * width,
                        "p (k c) -> p k c", {"k": n})

            def gu_src(l, h, f):
                return w_gate_up[l, :, h * FF:(h + 1) * FF].rearrange("(k p) c -> p k c", p=P)[:, :, bass.ds(f * P, P)]

            for l, seg in ORDER:
                u0 = UNIT0[(l, seg)]
                if seg in MOD_BLOCKS:
                    for i, b in enumerate(MOD_BLOCKS[seg]):
                        m = BLOCK0[(l, seg)] + i
                        if m >= 2:
                            sp.wait_ge(mod_out, sum(MOD_OUT[MOD_KEYS[m - 2]]))
                        sp.dma_start(mod_row[2:3, m % 2, :], b_mod[l:l + 1, b * 512:(b + 1) * 512]).then_inc(bias_row_in[m % 2], 16)
                        for h in range(2):
                            send(u0 + 2 * i + h, rows(w_mod[l], 4 * h, 4, b * 512, 512))
                elif seg == "win":
                    for b in range(4):
                        for h in range(2):
                            send(u0 + 2 * b + h, rows(w_in[l], 4 * h, 4, b * 512, 512))
                    send(u0 + 8, rows(w_in[l], 0, 8, 2048, 256))
                elif seg == "wout":
                    for i in range(4):
                        send(u0 + i, rows(w_out[l], 4 * (i % 2), 4, (i // 2) * 512, 512))
                elif seg[:2] == "gu":
                    f0 = HALF * int(seg[2])
                    dst = [stage[:, q, :].rearrange("p (k g c) -> p k g c", k=KC, g=2) for q in range(2)]

                    def send_gu(e, f):
                        for h in range(2):
                            sp.dma_start(dst[(u0 + e) % 2][:, :, h, :], gu_src(l, h, f)).then_inc(unit_in[(u0 + e) % 2], 16)

                    for g in range(2):
                        unit_release_wait(sp, u0 + g - 2)
                        send_gu(g, f0 + g)
                    with sp.Fori(1, HALF // 2) as i:
                        for e in range(2):
                            sp.wait_ge(w_ready, i * 8 + (SLOT0[(l, seg)] - 8 + 4 * (e + 1)))
                            send_gu(e, i * 2 + (f0 + e))
                    unit_release_wait(sp, u0 + HALF - 3)
                    send_gu(HALF - 1, f0 + HALF - 1)
                else:
                    f0 = HALF * int(seg[2])
                    for i in range(6):
                        k0 = f0 + 4 * (i % 3)
                        send(u0 + i, rows(w_down[l], k0, SEGMENTS[seg][i], (i // 3) * 512, 512))

            for n, t in enumerate(LAT):
                sp.wait_ge(sem("x_ready"), n + 1)
                sp.dma_start(out[0, (t - CT) * P:(t - CT + 1) * P, :], X[:, t, :]).then_inc(sem("out_sent"), 16)
            sp.wait_ge(sem("out_sent"), 16 * len(LAT))

        @block.gpsimd
        def _(pool):
            def split(g, par, j, n_hi):
                nc.gpsimd.tensor_scalar(ring_hi[:, g % RING, :], stage[:, par, j * 512:(j + 1) * 512], 1.0, 0.0,
                                        ALU.mult, ALU.add).then_inc(w_hi, 1)
                pool.wait_ge(w_hi, n_hi)
                nc.gpsimd.tensor_tensor(ring_lo[:, g % RING, :], stage[:, par, j * 512:(j + 1) * 512],
                                        ring_hi[:, g % RING, :].bitcast(F32), ALU.subtract).then_inc(w_ready, 1)

            def mod_terms(item, k):
                l, seg, i = item
                u, n = UNIT0[(l, seg)] + 2 * i + k // 4, POOL_NO[item]
                if k % 4 == 0:
                    unit_wait(pool, u)
                if k == 0 and FILL_NO[item] >= 2:
                    pool.wait_ge(mod_summed, FILL_NO[item] - 1)
                sums, tmp = partial_sums(item)
                acc = sums[:, 1, :]
                nc.gpsimd.tensor_scalar(tmp if k else acc, stage[:, u % 2, (k % 4) * 512:(k % 4 + 1) * 512],
                                        c_silu[:, 1, k:k + 1], 0.0, ALU.mult, ALU.add).then_inc(mod_product, 1)
                pool.wait_ge(mod_product, KC * n + k + 1)
                if k:
                    nc.gpsimd.tensor_tensor(acc, acc, tmp, ALU.add).then_inc(mod_added, 1)
                    pool.wait_ge(mod_added, (KC - 1) * n + k)

            def pads(l):
                items, rets = attn_items(l), ret_items(l)
                need(pool, "qk_read", l, sum(len(block_tiles(l, b)) for b in range(4)))
                for a in range(2):
                    other = slice((1 - a) * HD, (1 - a) * HD + HD)
                    z = nc.gpsimd.memset(padded[other, 2 * a:2 * a + 2, :], 0.0)
                need(pool, "pre_ready", l, pre_count(l, 4, len(block_tiles(l, 4)) - 1))
                for a in range(2):
                    z = nc.gpsimd.memset(q_pad_ret[slice((1 - a) * HD, (1 - a) * HD + HD), a, :], 0.0)
                z.then_inc(sem("pad_zero"), 1)
                need(pool, "pad_zero", l, 1)
                pool.wait_ge(c_ready, 1)
                fill = attn_fill(l)
                for i, (g, t, h, _) in enumerate(items):
                    rows = slice((h // 2) * HD, (h // 2) * HD + HD)
                    if i >= 4:
                        need(pool, "scores_ready", l, i - 3)
                    nc.gpsimd.tensor_scalar(padded[rows, h, :], qk_attn[g][rows, h % 2, t * P:(t + 1) * P], 1.0, 0.0,
                                            ALU.mult, ALU.add).then_inc(sem("q_pad"), 1)
                    if i // 8 < len(fill):
                        need(pool, "q_pad", l, i + 1)
                        mod_terms(fill[i // 8], i % 8)
                need(pool, "scores_ready", l, len(items))
                fill = ret_fill(l)

                def ret_pad(h):
                    rows = slice((h % 2) * HD, (h % 2) * HD + HD)
                    if h >= 2:
                        need(pool, "ret_scores", l, (h - 1) * (len(rets) // 4))
                    cols = slice(0 if l < DEPTH - 1 else CTX, TOK)
                    nc.gpsimd.tensor_scalar(q_pad_ret[rows, h % 2, cols], q_ret[rows, h // 2, cols], 1.0, 0.0,
                                            ALU.mult, ALU.add).then_inc(sem("ret_q_pad"), 1)
                    need(pool, "ret_q_pad", l, h + 1)

                ret_pad(0)
                ret_pad(1)
                for h in range(4):
                    if h < len(fill):
                        for k in range(KC):
                            mod_terms(fill[h], k)
                    if h + 2 < 4:
                        ret_pad(h + 2)

            def norm_low(key, n, t):
                c = slice(t * P, (t + 1) * P)
                need(pool, "h_hi", key, n + 1)
                nc.gpsimd.tensor_tensor(act_lo[:, :, c], hbuf[:, n % 2, :].rearrange("p (k t) -> p k t", k=KC),
                                        act_hi[:, :, c].bitcast(F32), ALU.subtract).then_inc(sem("act_ready"), 1)

            norm_before = {(l, "win"): ("pre", 0) if l == 0 else (l - 1, 2) for l in range(DEPTH)}
            norm_before.update({(l, "gu0"): (l, 1) for l in range(DEPTH)})

            for l, seg in ORDER:
                u0, g0 = UNIT0[(l, seg)], SLOT0[(l, seg)]
                if seg == "wout":
                    pads(l)
                if seg == "modC":
                    need(pool, "hid_ready", l, HALF - 2)
                    for item in ffn_fill(l):
                        if not on_vector(item):
                            for k in range(KC):
                                mod_terms(item, k)
                if seg in MOD_BLOCKS:
                    continue
                lows = []
                if (l, seg) in norm_before:
                    key = norm_before[(l, seg)]
                    tiles = tiles_of(key[0]) if key[0] != "pre" else ALL
                    lows = [(key, n, t) for n, t in enumerate(tiles[:-2])]
                    while len(lows) > 1:
                        norm_low(*lows.pop(0))
                for n in SEGMENTS[seg]:
                    unit_wait(pool, u0)
                    for j in range(n):
                        if g0 >= RING:
                            pool.wait_ge(ring_used, g0 - 7)
                        split(g0, u0 % 2, j, g0 + 1)
                        g0 += 1
                        if lows and j % 2:
                            norm_low(*lows.pop(0))
                    u0 += 1

        @block.tensor
        def _(pe):
            def product(o, a_hi, a_lo, b_hi, b_lo, first, last):
                nc.tensor.matmul(o, a_hi, b_hi, start=first, stop=False)
                nc.tensor.matmul(o, a_hi, b_lo, start=False, stop=False)
                return nc.tensor.matmul(o, a_lo, b_hi, start=False, stop=last)

            def mod_segment(l, seg):
                for i, b in enumerate(MOD_BLOCKS[seg]):
                    m = BLOCK0[(l, seg)] + i
                    if m >= 2:
                        pe.wait_ge(mod_row_ready, m - 1)
                    for h in range(2):
                        u = UNIT0[(l, seg)] + 2 * i + h
                        unit_wait(pe, u)
                        for k in range(4):
                            mm = nc.tensor.matmul(ps[0:2, m % 2, :], c_silu[:, :, 4 * h + k],
                                                  stage[:, u % 2, k * 512:(k + 1) * 512],
                                                  start=(4 * h + k == 0), stop=(4 * h + k == 7))
                        mm.then_inc(mod_used, 1)
                    pe.wait_ge(mod_row_ready, m + 1)
                    pe.wait_ge(bias_row_in[m % 2], 16 * (m // 2 + 1))
                    n, k = MOD_OUT[(l, seg, i)]
                    for o in range(k):
                        if n + o >= 2:
                            pe.wait_ge(mod_out_read, n + o - 1)
                        bank = 2 + (n + o) % 2
                        if seg in ("modA", "modB"):
                            for q in range(4):
                                mm = nc.tensor.matmul(ps[:, bank, 2 * q:2 * q + 2], mod_row[:, m % 2, q * P:(q + 1) * P],
                                                      sel[:, 0:2], start=True, stop=True)
                        else:
                            mm = nc.tensor.matmul(ps[:, bank, :], sel[:, o:o + 1].to_broadcast([3, P]), mod_row[:, m % 2, :],
                                                  start=True, stop=True)
                        mm.then_inc(mod_out, 1)

            def mod_sums(item, bank):
                l, seg, i = item
                m = BLOCK0[(l, seg)] + i
                pe.wait_ge(mod_partial, KC * (FILL_NO[item] + 1))
                if not on_vector(item):
                    pe.wait_ge(mod_added, (KC - 1) * (POOL_NO[item] + 1))
                pe.wait_ge(mod_row_ready, m)
                for o in range(2):
                    mm = nc.tensor.matmul(ps[0:2, bank, :], pick[:, o, :], partial_sums(item)[0][:, o, :], start=(o == 0), stop=(o == 1))
                mm.then_inc(mod_summed, 1)

            def mod_columns(item, bank):
                l, seg, i = item
                m = BLOCK0[(l, seg)] + i
                pe.wait_ge(mod_row_ready, m + 1)
                pe.wait_ge(bias_row_in[m % 2], 16 * (m // 2 + 1))
                pe.wait_ge(mod_out_read, MOD_OUT[item][0])
                for q in range(4):
                    mm = nc.tensor.matmul(ps[:, bank, P + 2 * q:P + 2 * q + 2], mod_row[:, m % 2, q * P:(q + 1) * P], sel[:, 0:2],
                                          start=True, stop=True)
                mm.then_inc(mod_out, 1)

            def mod_gates(l, seg):
                for i in range(len(MOD_BLOCKS[seg])):
                    m = BLOCK0[(l, seg)] + i
                    n, k = MOD_OUT[(l, seg, i)]
                    pe.wait_ge(mod_row_ready, m + 1)
                    pe.wait_ge(bias_row_in[m % 2], 16 * (m // 2 + 1))
                    for o in range(k):
                        pe.wait_ge(mod_out_read, n + o - 1)
                        nc.tensor.matmul(ps[:, 2 + (n + o) % 2, :], sel[:, o:o + 1].to_broadcast([3, P]), mod_row[:, m % 2, :],
                                         start=True, stop=True).then_inc(mod_out, 1)

            def transposes(key, n):
                need(pe, "xn_ready", key, n + 1)
                if n > 0:
                    need(pe, "h_ready", key, n)
                    if shared_modulation(key, n - 1):
                        nt = NT if key[0] == "pre" else len(tiles_of(key[0]))
                        need(pe, "h_half", key, signals("h_half", key) - (nt - n))
                for k in range(KC):
                    mm = nc.tensor.transpose(ps[:, 6 + k // 4, (k % 4) * P:(k % 4 + 1) * P], xn[:, n % 2, k * P:(k + 1) * P],
                                             ident[:, :])
                mm.then_inc(sem("xn_T"), 1)

            def project(l):
                g = SLOT0[(l, "win")]
                key = ("pre", 0) if l == 0 else (l - 1, 2)
                tp = [0]

                def tpose(b, n, t):
                    chunks = {0: 3, 1: 3, 2: 4, 3: 2}[b]
                    need(pe, "post_ready", l, pre_count(l, b, n))
                    if tp[0] >= 2:
                        need(pe, "qk_read", l, tp[0] - 1)
                    for k in range(chunks):
                        src = post[:, tp[0] % 2, k * P:(k + 1) * P]
                        mm = nc.tensor.transpose(ps[:, 6 + tp[0] % 2, k * P:(k + 1) * P], src, ident[:, :])
                    mm.then_inc(sem("qk_T"), 1)
                    tp[0] += 1

                for b in range(5):
                    tiles = block_tiles(l, b)
                    width, ks, slots = (512, 1, 8) if b < 4 else (256, 2, 4)
                    for j in range(slots):
                        pe.wait_ge(w_ready, g + 1)
                        for n, t in enumerate(tiles):
                            if j == 0 and b == 0:
                                wait_low(pe, key, n)
                            elif j == 0:
                                pb = block_tiles(l, b - 1)
                                if t in pb:
                                    need(pe, "pre_ready", l, pre_count(l, b - 1, pb.index(t)))
                                else:
                                    pb = block_tiles(l, b - 2)
                                    need(pe, "pre_ready", l, pre_count(l, b - 2, pb.index(t)))
                            for q in range(ks):
                                k = ks * j + q
                                s = slice(t * P, (t + 1) * P)
                                w = slice(q * width, (q + 1) * width)
                                mm = product(ps[:, t, 0:width], act_hi[:, k, s], act_lo[:, k, s],
                                             ring_hi[:, g % RING, w], ring_lo[:, g % RING, w], k == 0, k == KC - 1)
                            if n == len(tiles) - 1:
                                mm.then_inc(ring_used, 1)
                            elif j == slots - 1:
                                mm.then_inc(sem("win_acc"), 1)
                        g += 1
                        if 0 < b < 4 and j >= 2:
                            pt = block_tiles(l, b - 1)
                            if j - 2 < len(pt):
                                tpose(b - 1, j - 2, pt[j - 2])
                for n, t in enumerate(block_tiles(l, 3)):
                    tpose(3, n, t)

            def attention(l):
                items = attn_items(l)
                tiles = tiles_of(l)
                total = len(items)

                def scores(i):
                    g, t, h, keys = items[i]
                    q = padded[:, h, :]
                    kT = qk_attn[g]
                    need(pe, "q_pad", l, i + 1)
                    bank = 2 * (i % 2)
                    if i >= 2:
                        need(pe, "probs_ready", l, i - 1)
                    runs, col = [], 0
                    for k in keys:
                        if runs and runs[-1][1] + runs[-1][2] == k and (col // 512 == runs[-1][0] // 512):
                            runs[-1][2] += 1
                        else:
                            runs.append([col, k, 1])
                        col += P
                    flat = ps[:, bank:bank + 2, :].rearrange("p b n -> p (b n)")
                    for r, (c0, k0, m) in enumerate(runs):
                        edge = g == "B" and t >= CT
                        masks = [(kk, 0 if kk < t else 1) for kk in range(k0, k0 + m) if edge and kk >= CT and kk != t]
                        mm = nc.tensor.matmul(flat[:, c0:c0 + m * P], q, kT[:, 2, k0 * P:(k0 + m) * P],
                                              start=True, stop=not masks, skip_group_check=True)
                        for a, (kk, which) in enumerate(masks):
                            o = c0 + (kk - k0) * P
                            mm = nc.tensor.matmul(flat[:, o:o + P], ident[:, :], mask[:, which, :],
                                                  start=False, stop=(a == len(masks) - 1), skip_group_check=True)
                    mm.then_inc(sem("scores_ready"), 1)

                def transpose_probs(i):
                    _, _, _, keys = items[i]
                    need(pe, "probs_ready", l, i + 1)
                    if i >= 1:
                        need(pe, "probs_T_ready", l, i)
                        n = sum(len(items[a][3]) > 4 for a in range(i))
                        if n:
                            need(pe, "probs_T2_ready", l, n)
                    flat = ps[:, 4:6, :].rearrange("p b n -> p (b n)")
                    for k in range(len(keys)):
                        mm = nc.tensor.transpose(flat[:, k * P:(k + 1) * P], probs[:, i % 3, k * P:(k + 1) * P], ident[:, :])
                    mm.then_inc(sem("probs_T_done"), 1)

                def values(i):
                    g, t, h, keys = items[i]
                    need(pe, "probs_T_ready", l, i + 1)
                    n = sum(len(items[a][3]) > 4 for a in range(i + 1))
                    if n:
                        need(pe, "probs_T2_ready", l, n)
                    if i >= 1:
                        need(pe, "o_read", l, i)
                    for a, k in enumerate(keys):
                        mm = nc.tensor.matmul(ps[:, 6, 0:HD], probs_T[:, i % 2, a * P:(a + 1) * P],
                                              v_attn[g][:, k, (h // 2) * HD:(h // 2 + 1) * HD],
                                              start=(a == 0), stop=(a == len(keys) - 1))
                    mm.then_inc(sem("values_done"), 1)

                def out_T(q):
                    need(pe, "o_read", l, 4 * q + 4)
                    i, r = divmod(4 * q + 7, 8)
                    if 0 < i <= len(fill):
                        pe.wait_ge(mod_row_ready, BLOCK0[fill[i - 1][:2]] + fill[i - 1][2] + 1)
                        if r == 7:
                            pe.wait_ge(mod_out_read, MOD_OUT[fill[i - 1]][0] + 1)
                    for k in range(2):
                        mm = nc.tensor.transpose(ps[:, 7, 256 + k * P:256 + (k + 1) * P], o_attn[:, q % 2, k * P:(k + 1) * P], ident[:, :])
                    mm.then_inc(sem("o_T"), 1)

                fill = attn_fill(l)
                for s in range(total + 5):
                    if s < total:
                        scores(s)
                    if 2 <= s < total + 2:
                        transpose_probs(s - 2)
                    if 3 <= s < total + 3:
                        values(s - 3)
                    if s >= 4 and (s - 4) % 4 == 3 and s - 4 < total:
                        out_T((s - 4) // 4)
                    i, q = divmod(s, 8)
                    if q in (2, 4) and 0 < i <= len(fill):
                        need(pe, "o_T_lo", l, (s - 3) // 4)
                        (mod_sums if q == 2 else mod_columns)(fill[i - 1], 7)

            def retention(l):
                items = ret_items(l)
                per = len(items) // 4
                need_ctx = l < DEPTH - 1
                n_t = len(tiles_of(l))

                def scores(i):
                    h, s, lat = items[i]
                    cols = slice(CTX, TOK) if lat else slice(0, CTX)
                    need(pe, "ret_q_pad", l, h + 1)
                    if i >= 2:
                        need(pe, "decayed_ready", l, i - 1)
                    elif i == 0:
                        need(pe, "probs_ready", l, len(attn_items(l)))
                    mm = nc.tensor.matmul(ps[:, i % 2, 0:cols.stop - cols.start], k_ret[:, h // 2, s * P:(s + 1) * P],
                                          q_pad_ret[:, h % 2, cols], start=True, stop=True)
                    mm.then_inc(sem("ret_scores"), 1)

                def values(i):
                    h, s, lat = items[i]
                    need(pe, "decayed_ready", l, i + 1)
                    first = i % per == 0
                    if first and h >= 2:
                        need(pe, "o_ret_ready", l, h - 1)
                    queries = range(4) if lat else range(2)
                    for a in queries:
                        col = (a if lat else 4 + a) * HD
                        mm = nc.tensor.matmul(ps[:, 2 + h % 2, col:col + HD], decayed[:, i % 2, a * P:(a + 1) * P],
                                              v_ret[:, s, h * HD:(h + 1) * HD], start=(first and a == 0),
                                              stop=(i % per == per - 1 and a == queries[-1]), skip_group_check=True)
                    mm.then_inc(sem("ret_values"), 1)

                fill = ret_fill(l)
                for s in range(len(items) + 2):
                    if s < len(items):
                        scores(s)
                    if s >= 2:
                        values(s - 2)
                    i, q = divmod(s, 8)
                    if q == 1 and 0 < i <= len(fill):
                        mod_sums(fill[i - 1], 5)
                    if q == 3 and 0 < i <= len(fill) and fill[i - 1][1] != "modG":
                        mod_columns(fill[i - 1], 6)

            def fourier(l):
                need_ctx = l < DEPTH - 1
                tiles = tiles_of(l)
                need(pe, "four_in", l, 16 * (7 if need_ctx else 6))
                need(pe, "o_T_lo", l, len(tiles) * 2)
                pe.wait_ge(mod_row_ready, BLOCK0[(l, "modG")] + 2)
                pe.wait_ge(mod_out_read, MOD_OUT[(l, "modG", 0)][0])
                for ch in range(2):
                    for w in range(2):
                        mm = nc.tensor.matmul(ps[:, 4, ch * 256 + w * P:ch * 256 + (w + 1) * P], chan[:, w, :], mix_bd[:, ch, :],
                                              start=True, stop=True)
                mm.then_inc(sem("g_done"), 1)
                need(pe, "g_ready", l, 1)
                for n, t in enumerate(tiles):
                    if n >= 2:
                        need(pe, "ab_ready", l, n - 1)
                    for ch in range(2):
                        mm = nc.tensor.matmul(ps[:, 4 + (n + 1) % 2, ch * 256:(ch + 1) * 256], u_four[:, ch, t * P:(t + 1) * P],
                                              g_mat[:, ch, :], start=True, stop=True)
                    mm.then_inc(sem("ab_done"), 1)
                need(pe, "ab_ready", l, len(tiles))
                need(pe, "decayed_ready", l, len(ret_items(l)))
                for ch in range(2):
                    n = 0
                    for t in LAT:
                        for w in range(2):
                            o = ch * 256 + w * P
                            mm = nc.tensor.matmul(ps[:, 6 + ch, :], four_ab[:, t, o:o + P], dft_lat[:, t - CT, w, :],
                                                  start=(n == 0), stop=(n == 7))
                            n += 1
                    mm.then_inc(sem("four_done"), 1)
                if need_ctx:
                    for ch in range(2):
                        n = 0
                        for t in range(CT):
                            for w in range(2):
                                o = ch * 256 + w * P
                                mm = nc.tensor.matmul(ps[:, ch, 0:CTX], four_ab[:, t, o:o + P], dft_ctx[:, t, w, :],
                                                      start=(n == 0), stop=(n == 3))
                                n += 1
                        mm.then_inc(sem("four_done"), 1)
                for n, t in enumerate(tiles):
                    need(pe, "y_ret_ready", l, n + 1)
                    if n >= 2:
                        need(pe, "y_lo", l, n - 1)
                    for k in range(2):
                        mm = nc.tensor.transpose(ps[:, 4 + n % 2, k * P:(k + 1) * P], o_ret[:, t, k * P:(k + 1) * P], ident[:, :])
                    mm.then_inc(sem("y_T"), 1)

            def mix_out(l):
                tiles = tiles_of(l)
                nt = len(tiles)
                key = (l, 1)
                g = SLOT0[(l, "wout")]
                need(pe, "y_lo", l, nt)
                need(pe, "four_lo", l, 4 if l < DEPTH - 1 else 2)
                pe.wait_ge(mod_out_read, mod_done(l, "modG"))
                for j in range(8):
                    pe.wait_ge(w_ready, g + 1)
                    for n, t in enumerate(tiles):
                        s = slice(t * P, (t + 1) * P)
                        mm = product(ps[:, t, :], act_hi[:, j, s], act_lo[:, j, s], ring_hi[:, g % RING, :],
                                     ring_lo[:, g % RING, :], j == 0, j == 7)
                        if n == nt - 1:
                            mm.then_inc(ring_used, 1)
                        elif j == 7:
                            mm.then_inc(sem("wout_acc"), 1)
                    g += 1
                last_pass(l, key, tiles, "wout", 1, g, 8, lambda j, s: (act_hi[:, j, s], act_lo[:, j, s]), None)

            def last_pass(l, key, tiles, seg, p, g, m, left, ready):
                nt = len(tiles)
                for n, t in enumerate(tiles):
                    s = slice(t * P, (t + 1) * P)
                    if m == 8:
                        need(pe, seg + "_read", l, (p - 1) * nt + n + 1)
                    for j in range(8):
                        if n == 0:
                            pe.wait_ge(w_ready, g + j + 1)
                            if ready:
                                ready(j)
                        a_hi, a_lo = left(j, s)
                        mm = product(ps[:, t, :], a_hi, a_lo, ring_hi[:, (g + j) % RING, :],
                                     ring_lo[:, (g + j) % RING, :], j == 0 and m == 8, j == 7)
                        if n == nt - 1:
                            mm.then_inc(ring_used, 1)
                        elif j == 7:
                            mm.then_inc(sem(seg + "_acc"), 1)
                    if n >= 4 and key != (DEPTH - 1, 2):
                        transposes(key, n - 4)
                if key != (DEPTH - 1, 2):
                    for n in range(max(nt - 4, 0), nt):
                        transposes(key, n)

            def gate_up(l, fh):
                lo_col, width, parts = (0, 384, 2) if l < DEPTH - 1 else (CTX, 512, 1)
                seg = f"gu{fh}"
                g0 = SLOT0[(l, seg)]
                f0 = fh * HALF

                def chunk(g, f, slot_base, hid_base, first_pair):
                    bank = 4 * (f % 2)
                    if not first_pair:
                        need(pe, "hid_ready", l, hid_base)
                    for j in range(4):
                        pe.wait_ge(w_ready, slot_base + j)
                        for q in range(2):
                            k = 2 * j + q
                            for gu in range(2):
                                w = slice(q * 256 + gu * P, q * 256 + (gu + 1) * P)
                                wh, wl = ring_hi[:, (g + j) % RING, w], ring_lo[:, (g + j) % RING, w]
                                for r in range(parts):
                                    o = ps[:, bank + 2 * gu + r, 0:width]
                                    s = slice(lo_col + r * width, lo_col + (r + 1) * width)
                                    mm = product(o, wh, wl, act_hi[:, k, s], act_lo[:, k, s], k == 0, k == 7)
                        mm.then_inc(ring_used, 1)

                if fh == 0:
                    for n in (len(tiles_of(l)) - 3, len(tiles_of(l)) - 1):
                        wait_low(pe, (l, 1), n)
                else:
                    need(pe, "dn_read", l, 2 * len(tiles_of(l)))
                for f in range(2):
                    chunk(g0 + 4 * f, f, g0 + 4 * f + 1, None, True)
                with pe.Fori(1, HALF // 2) as i:
                    for e in range(2):
                        chunk(g0 + 4 * e, e, i * 8 + (g0 + 4 * e + 1), i * 2 + (f0 + e - 1), False)
                f = HALF - 1
                chunk(g0 + 4 * f, f, g0 + 4 * f + 1, f0 + f - 1, False)

            def down(l, fh):
                tiles = tiles_of(l)
                nt = len(tiles)
                for dh in range(2):
                    p = 2 * fh + dh
                    n_outer = 3 if p == 3 else HALF
                    for j in range(n_outer):
                        g = dn_slot(l, p, j)
                        pe.wait_ge(w_ready, g + 1)
                        need(pe, "hid_split", l, p * HALF + j + 1)
                        a_hi, a_lo = hid_slot(p, j)
                        for n, t in enumerate(tiles):
                            if j == 0:
                                if dh == 0:
                                    need(pe, "hid_ready", l, (fh + 1) * HALF)
                                else:
                                    need(pe, "dn_read", l, (p - 1) * nt + n + 1)
                            s = slice(t * P, (t + 1) * P)
                            mm = product(ps[:, t, :], a_hi[:, s], a_lo[:, s], ring_hi[:, g % RING, :],
                                         ring_lo[:, g % RING, :], j == 0, j == HALF - 1)
                            if n == nt - 1:
                                mm.then_inc(ring_used, 1)
                            elif j == HALF - 1:
                                mm.then_inc(sem("dn_acc"), 1)
                    if p == 3:
                        last_pass(l, (l, 2), tiles, "dn", 3, dn_slot(l, 3, 3), 11,
                                  lambda j, s: tuple(h[:, s] for h in hid_slot(3, 3 + j)),
                                  lambda j: need(pe, "hid_split", l, 3 * HALF + 3 + j + 1))

            pe.wait_ge(const_in, 16 * N_CONST)
            pe.wait_ge(sem("c_row_ready"), 1)
            nc.tensor.transpose(ps[:, 0, 0:2 * KC], c_row[:, :], ident[0:2 * KC, 0:2 * KC]).then_inc(sem("c_T"), 1)
            pe.wait_ge(c_ready, 1)
            mod_segment(0, "modA")
            for n in range(NT):
                transposes(("pre", 0), n)
            for l in range(DEPTH):
                tiles = tiles_of(l)
                project(l)
                need(pe, "pre_ready", l, pre_count(l, 4, len(tiles) - 1))
                need(pe, "qk_read", l, sum(len(block_tiles(l, b)) for b in range(4)))
                attention(l)
                retention(l)
                fourier(l)
                need(pe, "four_lo", l, 4 if l < DEPTH - 1 else 2)
                need(pe, "o_ret_ready", l, 4)
                mod_gates(l, "modG")
                mix_out(l)
                gate_up(l, 0)
                need(pe, "hid_ready", l, HALF)
                for i, item in enumerate(ffn_fill(l)):
                    mod_sums(item, i)
                mod_gates(l, "modC")
                pe.wait_ge(mod_out_read, mod_done(l, "modC"))
                down(l, 0)
                gate_up(l, 1)
                down(l, 1)

        @block.scalar
        def _(act):
            a = nc.scalar

            def mod_segment(l, seg):
                for i, b in enumerate(MOD_BLOCKS[seg]):
                    m = BLOCK0[(l, seg)] + i
                    n, k = MOD_OUT[(l, seg, i)]
                    if m >= 2:
                        act.wait_ge(mod_out, sum(MOD_OUT[MOD_KEYS[m - 2]]))
                    act.wait_ge(mod_used, UNITS[UNIT0[(l, seg)] + 2 * i + 1][3])
                    a.activation(mod_row[0:2, m % 2, :], ps[0:2, m % 2, :], ACT.Copy).then_inc(mod_row_ready, 1)
                    for o in range(k):
                        act.wait_ge(mod_out, n + o + 1)
                        bank = 2 + (n + o) % 2
                        if seg in ("modA", "modB"):
                            which = b // 2 if seg == "modA" else b // 2 - 1
                            dst = mod_col[:, which, 4 * (b % 2):4 * (b % 2) + 4, :]
                            a.activation(dst, ps[:, bank, 0:8].rearrange("p (k s) -> p k s", s=2), ACT.Copy).then_inc(mod_out_read, 1)
                        else:
                            a.activation(bc[:, o, (b % 2) * 512:(b % 2 + 1) * 512], ps[:, bank, :], ACT.Copy).then_inc(mod_out_read, 1)

            def mod_rows(item, bank):
                l, seg, i = item
                m = BLOCK0[(l, seg)] + i
                act.wait_ge(mod_out, sum(MOD_OUT[MOD_KEYS[m - 2]]))
                act.wait_ge(mod_summed, FILL_NO[item] + 1)
                a.activation(mod_row[0:2, m % 2, :], ps[0:2, bank, :], ACT.Copy).then_inc(mod_row_ready, 1)

            def mod_columns(item, bank):
                l, seg, i = item
                act.wait_ge(mod_out, MOD_OUT[item][0] + 1)
                b = MOD_BLOCKS[seg][i]
                which = b // 2 if seg == "modA" else b // 2 - 1
                a.activation(mod_col[:, which, 4 * (b % 2):4 * (b % 2) + 4, :],
                             ps[:, bank, P:P + 8].rearrange("p (k s) -> p k s", s=2), ACT.Copy).then_inc(mod_out_read, 1)

            def mod_gates(l, seg):
                for i, b in enumerate(MOD_BLOCKS[seg]):
                    n, k = MOD_OUT[(l, seg, i)]
                    for o in range(k):
                        act.wait_ge(mod_out, n + o + 1)
                        a.activation(bc[:, o, (b % 2) * 512:(b % 2 + 1) * 512], ps[:, 2 + (n + o) % 2, :],
                                     ACT.Copy).then_inc(mod_out_read, 1)

            def norm_steps(key, tiles):
                last = key == (DEPTH - 1, 2)
                nt = len(tiles)
                which = 0 if key[1] != 1 else 1
                if not last:
                    need(act, "scale_plus_1", key, 1)
                for step in range(nt + 5):
                    for s in (5, 3, 4, 2, 1) if key[0] == "pre" or step > nt else (5, 4, 3, 2, 1):
                        n = step - s + 1
                        if not 0 <= n < nt:
                            continue
                        t = tiles[n]
                        stream = 0 if t >= CT else 1
                        if s == 1 and key[0] != "pre":
                            need(act, "var1", key, n + 1)
                            a.activation(st[:, t, 14:15], st[:, t, 13:14], ACT.Sqrt, bias=eps[:, :]).then_inc(sem("sd1"), 1)
                        elif s == 2 and not last:
                            need(act, "var2", key, n + 1)
                            a.activation(st[:, t, 31:32], st[:, t, 30:31], ACT.Sqrt, bias=eps[:, :]).then_inc(sem("sd2"), 1)
                        elif s == 3 and not last:
                            need(act, "scale2", key, n + 1)
                            if n >= 2:
                                need(act, "xn_T", key, n - 1)
                            a.activation(xn[:, n % 2, :], X[:, t, :], ACT.Identity, bias=st[:, t, 33:34],
                                         scale=st[:, t, 32:33]).then_inc(sem("xn_ready"), 1)
                        elif s == 4 and not last:
                            need(act, "xn_T", key, n + 1)
                            if n >= 2:
                                wait_low(act, key, n - 2)
                            for k in range(4 if shared_modulation(key, n) else 0, KC):
                                ins = a.activation(hbuf[:, n % 2, k * P:(k + 1) * P], ps[:, 6 + k // 4, (k % 4) * P:(k % 4 + 1) * P],
                                                   ACT.Identity, bias=mod_col[:, 2 * which, k, stream:stream + 1],
                                                   scale=mod_col[:, 2 * which + 1, k, stream:stream + 1])
                            ins.then_inc(sem("h_ready"), 1)
                        elif s == 5 and not last:
                            need(act, "h_ready", key, n + 1)
                            if shared_modulation(key, n):
                                need(act, "h_half", key, signals("h_half", key) - (nt - 1 - n))
                            a.activation(act_hi[:, :, t * P:(t + 1) * P], hbuf[:, n % 2, :].rearrange("p (k t) -> p k t", k=KC),
                                         ACT.Copy).then_inc(sem("h_hi"), 1)

            def project(l):
                tp = [0]

                def read_T(b, n, t):
                    need(act, "qk_T", l, tp[0] + 1)
                    src = ps[:, 6 + tp[0] % 2, :].rearrange("p (k t) -> p k t", t=P)
                    s = slice(t * P, (t + 1) * P)
                    if b < 2:
                        ins = a.activation(qk_attn["AB"[b]][:, :, s], src[:, 0:3, :], ACT.Copy)
                    elif b == 2:
                        a.activation(u_four[:, :, s], src[:, 0:2, :], ACT.Copy)
                        ins = a.activation(q_ret[:, :, s], src[:, 2:4, :], ACT.Copy)
                    else:
                        ins = a.activation(k_ret[:, :, s], src[:, 0:2, :], ACT.Copy)
                    ins.then_inc(sem("qk_read"), 1)
                    tp[0] += 1

                for b in range(5):
                    if 0 < b < 4:
                        if b == 1:
                            for n, t in enumerate(ALL):
                                need(act, "ssq_ready", l, n + 1)
                                a.activation(rms[:, t, :], ssq[:, t, :], ACT.Sqrt, bias=eps[:, :], scale=1.0 / HD).then_inc(sem("rms_sd"), 1)
                        for n, t in enumerate(block_tiles(l, b - 1)):
                            read_T(b - 1, n, t)
                    tiles = block_tiles(l, b)
                    for n, t in enumerate(tiles):
                        if n == len(tiles) - 1:
                            act.wait_ge(ring_used, win_last_slot(l, b) + 1)
                        else:
                            need(act, "win_acc", l, sum(len(block_tiles(l, q)) - 1 for q in range(b)) + n + 1)
                        if 0 < b < 4:
                            need(act, "post_ready", l, pre_count(l, b - 1, len(block_tiles(l, b - 1)) - 1))
                        acc = ps[:, t, :]
                        if b < 2:
                            a.activation(v_attn["AB"[b]][:, t, :], acc[:, 384:512], ACT.Copy)
                            ins = a.activation(pre[:, t, 0:384], acc[:, 0:384], ACT.Copy)
                        elif b == 2:
                            ins = a.activation(pre[:, t, :], acc, ACT.Copy)
                        elif b == 3:
                            a.activation(v_ret[:, t, :], acc[:, 256:512], ACT.Copy)
                            ins = a.activation(pre[:, t, 0:256], acc[:, 0:256], ACT.Copy)
                        else:
                            ins = a.activation(gate_ret[:, t, :], acc[:, 0:256], ACT.Silu)
                        ins.then_inc(sem("pre_ready"), 1)
                for n, t in enumerate(block_tiles(l, 3)):
                    read_T(3, n, t)

            def attention(l):
                items = attn_items(l)
                total = len(items)

                def probabilities(i):
                    g, t, h, keys = items[i]
                    n = len(keys) * P
                    need(act, "neg_ready", l, i + 1)
                    if i >= 3:
                        need(act, "probs_T_done", l, i - 2)
                    flat = ps[:, 2 * (i % 2):2 * (i % 2) + 2, :].rearrange("p b n -> p (b n)")
                    if g == "B":
                        a.activation(expsink[:, i % 4:i % 4 + 1], negmax[:, i % 4:i % 4 + 1], ACT.Exp, bias=sink[:, h:h + 1])
                    a.activation(probs[:, i % 3, 0:n], flat[:, 0:n], ACT.Exp, bias=negmax[:, i % 4:i % 4 + 1], scale=0.125,
                                 accum_out=expsum[:, i % 4:i % 4 + 1]).then_inc(sem("probs_ready"), 1)

                def read_T2(i):
                    g, t, h, keys = items[i]
                    if len(keys) <= 4:
                        return
                    need(act, "probs_T_done", l, i + 1)
                    if i >= 2:
                        need(act, "values_done", l, i - 1)
                    n = (len(keys) - 4) * P
                    a.activation(probs_T[:, i % 2, 512:512 + n], ps[:, 5, 0:n], ACT.Copy).then_inc(sem("probs_T2_ready"), 1)

                def out_hi(q):
                    g, t, _, _ = items[4 * q]
                    need(act, "o_T", l, q + 1)
                    ch = 0 if g == "A" else 2
                    a.activation(act_hi[:, ch:ch + 2, t * P:(t + 1) * P], ps[:, 7, 256:512].rearrange("p (k t) -> p k t", t=P),
                                 ACT.Copy).then_inc(sem("o_hi"), 1)

                fill = attn_fill(l)
                for s in range(total + 5):
                    if s < total:
                        probabilities(s)
                    if 2 <= s < total + 2:
                        read_T2(s - 2)
                    if s >= 4 and (s - 4) % 4 == 3 and s - 4 < total:
                        out_hi((s - 4) // 4)
                    i, q = divmod(s, 8)
                    if q in (2, 4) and 0 < i <= len(fill):
                        (mod_rows if q == 2 else mod_columns)(fill[i - 1], 7)

            def retention(l):
                items = ret_items(l)
                per = len(items) // 4
                need_ctx = l < DEPTH - 1
                need(act, "lg_set", l, 1)
                need(act, "delta_in", l, 16)

                def strips(h):
                    if h >= 2:
                        need(act, "decayed_ready", l, per * (h - 1))
                    a.activation(strip_ctx[:, h % 2, :], delta[:, 512:1152], ACT.Exp, scale=lg[:, 0, h:h + 1]).then_inc(sem("strip_exp"), 1)
                    if h >= 1:
                        need(act, "strip_ready", l, h)
                    a.activation(ctx_part[:, :], delta[:, 384:1024], ACT.Exp, scale=lg[:, 1, h:h + 1],
                                 bias=lg[:, 2, h:h + 1]).then_inc(sem("strip_exp"), 1)
                    need(act, "strip_arg", l, h + 1)
                    a.activation(strip[:, h % 2, :], strip[:, h % 2, :], ACT.Exp).then_inc(sem("strip_exp"), 1)

                def head_out(h):
                    need(act, "ret_values", l, per * (h + 1))
                    src = ps[:, 2 + h % 2, :].rearrange("p (t v) -> p t v", v=HD)
                    if need_ctx:
                        a.activation(o_ret[:, 0:CT, h * HD:(h + 1) * HD], src[:, 4:6, :], ACT.Copy, scale=0.125)
                    a.activation(o_ret[:, CT:NT, h * HD:(h + 1) * HD], src[:, 0:4, :], ACT.Copy, scale=0.125).then_inc(sem("o_ret_ready"), 1)

                strips(0)
                strips(1)
                fill = ret_fill(l)
                for h in range(4):
                    head_out(h)
                    if h + 2 < 4:
                        strips(h + 2)
                    if h < len(fill):
                        mod_rows(fill[h], 5)
                        if fill[h][1] != "modG":
                            mod_columns(fill[h], 6)

            def fourier(l):
                need_ctx = l < DEPTH - 1
                tiles = tiles_of(l)
                need(act, "ret_scores", l, len(ret_items(l)))
                act.dma_start(gn_w[:, :], r_gn_w[l].partition_broadcast(P)).then_inc(sem("gn_in"), 16)
                need(act, "g_done", l, 1)
                a.activation(g_mat[:, :, :], ps[:, 4, :].rearrange("p (c n) -> p c n", c=2), ACT.Copy).then_inc(sem("g_ready"), 1)
                need(act, "ret_values", l, len(ret_items(l)))

                for n, t in enumerate(tiles):
                    need(act, "ab_done", l, n + 1)
                    a.activation(four_ab[:, t, :], ps[:, 4 + (n + 1) % 2, :], ACT.Copy).then_inc(sem("ab_ready"), 1)
                need(act, "gvar", l, 1)
                a.activation(gsd[:, 0:len(tiles), :], gmv[:, 0:len(tiles), :, 1], ACT.Sqrt, bias=eps[:, :]).then_inc(sem("gsd"), 1)
                for ch in range(2):
                    need(act, "four_done", l, ch + 1)
                    a.activation(act_hi[:, 4 + ch, CTX:TOK], ps[:, 6 + ch, :], ACT.Copy).then_inc(sem("four_hi"), 1)
                if need_ctx:
                    for ch in range(2):
                        need(act, "four_done", l, 2 + ch + 1)
                        a.activation(act_hi[:, 4 + ch, 0:CTX], ps[:, ch, 0:CTX], ACT.Copy).then_inc(sem("four_hi"), 1)
                for n, t in enumerate(tiles):
                    need(act, "y_T", l, n + 1)
                    a.activation(act_hi[:, 6:8, t * P:(t + 1) * P], ps[:, 4 + n % 2, 0:256].rearrange("p (k t) -> p k t", t=P),
                                 ACT.Copy).then_inc(sem("y_hi"), 1)

            def load_norm(l, w, b):
                act.dma_start(bc[:, 2, :], w[l].partition_broadcast(P)).then_inc(sem("norm_in"), 16)
                act.dma_start(bc[:, 3, :], b[l].partition_broadcast(P)).then_inc(sem("norm_in"), 16)

            def gate_half(l, fh):
                width, parts = (384, 2) if l < DEPTH - 1 else (512, 1)
                lo_col = 0 if l < DEPTH - 1 else CTX
                g0 = SLOT0[(l, f"gu{fh}")]

                def chunk(e, done, free):
                    act.wait_ge(ring_used, done)
                    if free is not None:
                        need(act, "hid_ready", l, free)
                    ins = a.activation(silu_g[:, e, lo_col:TOK].rearrange("p (r n) -> p r n", r=parts),
                                       ps[:, 4 * e:4 * e + parts, 0:width], ACT.Silu)
                    ins.then_inc(sem("silu_ready"), 1)

                for e in range(2):
                    chunk(e, g0 + 4 * e + 4, None)
                with act.Fori(1, HALF // 2) as i:
                    for e in range(2):
                        chunk(e, i * 8 + (g0 + 4 * e + 4), i * 2 + (fh * HALF + e - 1))
                chunk(0, g0 + 4 * HALF, fh * HALF + HALF - 2)

            def down_hi(l, fh):
                cols = slice(0 if l < DEPTH - 1 else CTX, TOK)
                need(act, "hid_ready", l, (fh + 1) * HALF)
                for p in (2 * fh, 2 * fh + 1):
                    for j in range(HALF):
                        hid_slot_wait(act, l, p, j)
                        a.activation(hid_slot(p, j)[0][:, cols], hid[:, j, cols], ACT.Copy).then_inc(sem("hid_hi"), 1)

            act.dma_start(c_row[0:KC, :], c[0].rearrange("(k p) -> k p", p=P)).then_inc(c_in, 16)
            act.dma_start(c_row[KC:2 * KC, :], c_ctx.rearrange("(k p) -> k p", p=P)).then_inc(c_in, 16)
            act.dma_start(sel[:, :], tab["sel"]).then_inc(const_in, 16)
            act.dma_start(ident[:, :], tab["ident"]).then_inc(const_in, 16)
            act.dma_start(rope_seq[:, :, :, :], tab["rope_seq"]).then_inc(const_in, 16)
            act.dma_start(mask[:, :, :], tab["mask"]).then_inc(const_in, 16)
            act.dma_start(rope_grid[:, :, :, :], tab["rope_grid"]).then_inc(const_in, 16)
            act.dma_start(X[:, CT:NT, :], x[0].rearrange("(t p) d -> p t d", p=P)).then_inc(x_in, 16)
            act.dma_start(X[:, 0:CT, :], ctx_in[0].rearrange("(t p) d -> p t d", p=P)).then_inc(x_in, 16)
            act.wait_ge(c_in, 32)
            a.activation(c_row[:, :], c_row[:, :], ACT.Silu).then_inc(sem("c_row_ready"), 1)
            act.wait_ge(sem("c_T"), 1)
            a.activation(c_silu[:, :, :], ps[:, 0, 0:2 * KC].rearrange("p (s k) -> p s k", s=2), ACT.Copy).then_inc(c_ready, 1)
            mod_segment(0, "modA")
            act.wait_ge(x_in, 32)
            act.wait_ge(sem("eps_ready"), 1)
            norm_steps(("pre", 0), ALL)
            for l in range(DEPTH):
                tiles = tiles_of(l)
                nt = len(tiles)
                act.dma_start(qk_w[:, 0, :], a_q_norm[l].partition_broadcast(P)).then_inc(sem("qkw_in"), 16)
                act.dma_start(qk_w[:, 1, :], a_k_norm[l].partition_broadcast(P)).then_inc(sem("qkw_in"), 16)
                if l > 0:
                    act.dma_start(rope_grid[:, :, :, :], tab["rope_grid"]).then_inc(sem("qkw_in"), 16)
                    act.dma_start(rope_seq[:, :, :, :], tab["rope_seq"]).then_inc(sem("qkw_in"), 16)
                act.dma_start(sink[:, :], b_sink[l].partition_broadcast(P)).then_inc(sem("sink_in"), 16)
                act.dma_start(lg_raw[:, :], r_decay[l].rearrange("a b -> (a b)").partition_broadcast(P)).then_inc(sem("lg_in"), 16)
                project(l)
                need(act, "sink_in", l, 16)
                need(act, "lg_in", l, 16)
                a.activation(lg_raw[:, :], lg_raw[:, :], ACT.Exp, scale=-1.0).then_inc(sem("lg_exp"), 1)
                need(act, "lg_exp", l, 1)
                a.activation(lg_raw[:, :], lg_raw[:, :], ACT.Ln, bias=1.0).then_inc(sem("lg_ln"), 1)
                need(act, "post_ready", l, pre_count(l, 3, NT - 1))
                need(act, "qk_T", l, sum(len(block_tiles(l, b)) for b in range(4)))
                act.dma_start(delta[:, :], tab["delta"]).then_inc(sem("delta_in"), 16)
                attention(l)
                need(act, "values_done", l, len(attn_items(l)))
                need(act, "o_T", l, 2 * nt)
                act.dma_start(dft_lat[:, :, :, :], tab["dft_lat"]).then_inc(sem("four_in"), 16)
                if l < DEPTH - 1:
                    act.dma_start(dft_ctx[:, :, :, :], tab["dft_ctx"]).then_inc(sem("four_in"), 16)
                act.dma_start(chan[:, :, :], tab["chan"]).then_inc(sem("four_in"), 16)
                need(act, "mix_zero", l, 1)
                for g in range(4):
                    r = slice((g % 2) * HD, (g % 2) * HD + HD)
                    act.dma_start(mix_bd[r, g // 2, r], f_mix[l, g]).then_inc(sem("four_in"), 16)
                retention(l)
                fourier(l)
                need(act, "four_done", l, 4 if l < DEPTH - 1 else 2)
                load_norm(l, ln1_w, ln1_b)
                mod_gates(l, "modG")
                norm_steps((l, 1), tiles)
                load_norm(l, ln2_w, ln2_b)
                gate_half(l, 0)
                for i, item in enumerate(ffn_fill(l)):
                    mod_rows(item, i)
                mod_gates(l, "modC")
                down_hi(l, 0)
                gate_half(l, 1)
                down_hi(l, 1)
                norm_steps((l, 2), tiles)

        @block.vector
        def _(dve):
            v = nc.vector
            step_no = [0]

            def link(ins):
                step_no[0] += 1
                ins.then_inc(sem("dve_step"), 1)
                dve.wait_ge(sem("dve_step"), step_no[0])

            raised = {}

            def done(ins, name):
                raised[name] = raised.get(name, 0) + 1
                ins.then_inc(sem(name), 1)
                dve.wait_ge(sem(name), raised[name])

            def low(dst, src, high):
                return v.tensor_tensor(dst, src, high.bitcast(F32), ALU.subtract)

            def residual(l, seg, p, n, t, nt, last_slot, half, fresh):
                acc_wait(dve, l, seg, p, n, nt, last_slot)
                y = ps[:, t, :]
                cols = slice(half * 512, half * 512 + 512)
                link(v.tensor_tensor(y, y, bc[:, 0 if t >= CT else 1, cols], ALU.mult))
                if fresh:
                    ins = v.scalar_tensor_tensor(X[:, t, cols], X[:, t, cols], ALPHA, y, ALU.mult, ALU.add)
                else:
                    ins = v.tensor_tensor(X[:, t, cols], X[:, t, cols], y, ALU.add)
                done(ins, seg + "_read")

            def half_stats(t, o, h):
                return v.bn_stats(st[:, t, o + 6 * h:o + 6 * h + 6], X[:, t, h * 512:(h + 1) * 512])

            def variance(t, o, signal):
                done(v.bn_aggr(st[:, t, o + 12:o + 14], st[:, t, o:o + 12]), signal)

            def norm_steps(key, tiles, first):
                last = key == (DEPTH - 1, 2)
                which = 0 if key[1] != 1 else 1
                if not last:
                    seg = "modB" if which else "modA"
                    lay = 0 if key[0] == "pre" else (key[0] if which else key[0] + 1)
                    dve.wait_ge(mod_out_read, mod_done(lay, seg))
                    done(v.tensor_scalar_add(mod_col[:, 2 * which + 1, :, :], mod_col[:, 2 * which + 1, :, :], 1.0), "scale_plus_1")
                for step in range(len(tiles) + 4):
                    for s in (4, 2, 1, 0, 3):
                        n = step - s
                        if not 0 <= n < len(tiles):
                            continue
                        t = tiles[n]
                        if s == 4 and not last and n >= len(tiles) - 2:
                            need(dve, "h_hi", key, n + 1)
                            c = slice(t * P, (t + 1) * P)
                            done(low(act_lo[:, :, c], hbuf[:, n % 2, :].rearrange("p (k t) -> p k t", k=KC), act_hi[:, :, c]),
                                 "last_ready")
                        if s == 3 and not last and shared_modulation(key, n):
                            need(dve, "xn_T", key, n + 1)
                            if n >= 2:
                                wait_low(dve, key, n - 2)
                            stream = 0 if t >= CT else 1
                            for k in range(4):
                                ins = v.tensor_scalar(hbuf[:, n % 2, k * P:(k + 1) * P], ps[:, 6, k * P:(k + 1) * P],
                                                      mod_col[:, 2 * which + 1, k, stream:stream + 1],
                                                      mod_col[:, 2 * which, k, stream:stream + 1], ALU.mult, ALU.add)
                            done(ins, "h_half")
                        if s == 0 and first:
                            first(n, t)
                            link(half_stats(t, 0, 1))
                            variance(t, 0, "var1")
                        elif s == 1:
                            if first:
                                need(dve, "sd1", key, n + 1)
                                link(v.reciprocal(st[:, t, 15:16], st[:, t, 14:15]))
                                if n == 0:
                                    need(dve, "norm_in", key[0], 32 * key[1])
                                link(v.scalar_tensor_tensor(X[:, t, :], X[:, t, :], st[:, t, 12:13], bc[:, 2, :],
                                                            ALU.subtract, ALU.mult))
                                ins = v.scalar_tensor_tensor(X[:, t, :], X[:, t, :], st[:, t, 15:16], bc[:, 3, :],
                                                             ALU.mult, ALU.add)
                                if last:
                                    done(ins, "x_ready")
                                    continue
                                link(ins)
                            half_stats(t, 17, 0)
                            link(half_stats(t, 17, 1))
                            variance(t, 17, "var2")
                        elif s == 2 and not last:
                            need(dve, "sd2", key, n + 1)
                            link(v.reciprocal(st[:, t, 32:33], st[:, t, 31:32]))
                            done(v.scalar_tensor_tensor(st[:, t, 33:34], st[:, t, 29:30], -1.0, st[:, t, 32:33],
                                                        ALU.mult, ALU.mult), "scale2")

            def project(l):
                tp = [0]

                def by_head(q):
                    return q[:, 0:256].rearrange("p (a b d) -> p a b d", a=2, b=2)

                def by_key_head(q):
                    return q[:, 0:256].rearrange("p (b a d) -> p a b d", a=2, b=2)

                def rotate(dst, src, heads, grid, t):
                    table = (rope_grid if grid else rope_seq)[:, t - CT, :, :]
                    s3 = src.rearrange("p (h d) -> p h d", d=HD)
                    axes, part = (2, 16) if grid else (1, 32)
                    n = heads * HD
                    pat = "p (h a s d) -> p h a s d"
                    sw = dict(a=axes, s=2, d=part)
                    t5 = tmp2[:, 0:n].rearrange(pat, **sw)
                    s5 = src.rearrange(pat, **sw)
                    sin = table[:, 1, :].rearrange("p (a s d) -> p a s d", **sw)
                    for s in range(2):
                        ins = v.tensor_tensor(t5[:, :, :, s, :], s5[:, :, :, 1 - s, :],
                                              sin[:, :, s, :].unsqueeze(1).to_broadcast([P, heads, axes, part]), ALU.mult)
                    link(ins)
                    link(v.tensor_tensor(s3, s3, table[:, 0, :].unsqueeze(1).to_broadcast([P, heads, HD]), ALU.mult))
                    if heads == 6:
                        v.tensor_tensor(by_key_head(dst), by_head(src), by_head(tmp2), ALU.add)
                        return v.tensor_tensor(dst[:, 256:384], src[:, 256:384], tmp2[:, 256:384], ALU.add)
                    return v.tensor_tensor(dst, src, tmp2[:, 0:n], ALU.add)

                def arrange(b, n, t):
                    lat = t >= CT
                    o = post[:, tp[0] % 2, :]
                    if tp[0] >= 2:
                        need(dve, "qk_T", l, tp[0] - 1)
                    src = pre[:, t, :]
                    if b == 0:
                        need(dve, "rms_sd", l, n + 1)
                        link(v.reciprocal(ssq[:, t, :], rms[:, t, :]))
                        link(v.tensor_tensor(tmp1[:, 0:384].rearrange("p (h d) -> p h d", d=HD),
                                             src[:, 0:384].rearrange("p (h d) -> p h d", d=HD),
                                             ssq[:, t, :].unsqueeze(2).to_broadcast([P, 6, HD]), ALU.mult))
                        dst, q_to = (tmp1, by_head) if lat else (o, by_key_head)
                        v.tensor_tensor(q_to(dst), by_head(tmp1),
                                        qk_w[:, 0:1, :].unsqueeze(1).to_broadcast([P, 2, 2, HD]), ALU.mult)
                        ins = v.tensor_tensor(dst[:, 256:384].rearrange("p (h d) -> p h d", d=HD),
                                              tmp1[:, 256:384].rearrange("p (h d) -> p h d", d=HD),
                                              qk_w[:, 1:2, :].to_broadcast([P, 2, HD]), ALU.mult)
                        if lat:
                            link(ins)
                            ins = rotate(o[:, 0:384], tmp1[:, 0:384], 6, True, t)
                    elif b == 1:
                        if lat:
                            ins = rotate(o[:, 0:384], src[:, 0:384], 6, True, t)
                        else:
                            v.tensor_copy(by_key_head(o), by_head(src))
                            ins = v.tensor_copy(o[:, 256:384], src[:, 256:384])
                    elif b == 2:
                        if lat:
                            v.tensor_copy(o[:, 0:256], src[:, 0:256])
                            ins = rotate(o[:, 256:512], src[:, 256:512], 4, False, t)
                        else:
                            ins = v.tensor_copy(o, src)
                    else:
                        ins = rotate(o[:, 0:256], src[:, 0:256], 4, False, t) if lat else v.tensor_copy(o[:, 0:256], src[:, 0:256])
                    done(ins, "post_ready")
                    tp[0] += 1

                need(dve, "qkw_in", l, 32 if l == 0 else 64)
                for b in range(4):
                    tiles = block_tiles(l, b)
                    if b == 0:
                        for n, t in enumerate(tiles):
                            need(dve, "pre_ready", l, n + 1)
                            link(v.tensor_tensor(tmp2[:, 0:384], pre[:, t, 0:384], pre[:, t, 0:384], ALU.mult))
                            done(v.reduce_sum(ssq[:, t, :], tmp2[:, 0:384].rearrange("p (h d) -> p h d", d=HD), AX), "ssq_ready")
                    for n, t in enumerate(tiles):
                        need(dve, "pre_ready", l, pre_count(l, b, n))
                        arrange(b, n, t)

            def mod_terms(item, k):
                l, seg, i = item
                u = UNIT0[(l, seg)] + 2 * i + k // 4
                if k % 4 == 0:
                    unit_wait(dve, u)
                if k == 0 and FILL_NO[item] >= 2:
                    dve.wait_ge(mod_summed, FILL_NO[item] - 1)
                w = stage[:, u % 2, (k % 4) * 512:(k % 4 + 1) * 512]
                for o in range(2 if on_vector(item) else 1):
                    acc, c_k = partial_sums(item)[0][:, o, :], c_silu[:, o, k:k + 1]
                    if k == 0:
                        ins = v.tensor_scalar_mul(acc, w, c_k)
                    else:
                        ins = v.scalar_tensor_tensor(acc, w, c_k, acc, ALU.mult, ALU.add)
                done(ins, "mod_partial")

            def attention(l):
                items = attn_items(l)
                total = len(items)
                fill = attn_fill(l)

                def maxima(i):
                    g, t, h, keys = items[i]
                    need(dve, "scores_ready", l, i + 1)
                    flat = ps[:, 2 * (i % 2):2 * (i % 2) + 2, :].rearrange("p b n -> p (b n)")
                    m = slice(i % 4, i % 4 + 1)
                    link(v.reduce_max(rowmax[:, m], flat[:, 0:len(keys) * P], AX))
                    if g == "A":
                        ins = v.tensor_scalar_mul(negmax[:, m], rowmax[:, m], -0.125)
                    else:
                        ins = v.tensor_scalar(negmax[:, m], rowmax[:, m], -0.125, nsink[:, h:h + 1], ALU.mult, ALU.min)
                    done(ins, "neg_ready")

                def read_T(i):
                    g, t, h, keys = items[i]
                    need(dve, "probs_T_done", l, i + 1)
                    if i >= 2:
                        need(dve, "values_done", l, i - 1)
                    n = min(len(keys), 4) * P
                    done(v.tensor_copy(probs_T[:, i % 2, 0:n], ps[:, 4, 0:n]), "probs_T_ready")

                def output(i):
                    g, t, h, keys = items[i]
                    m = slice(i % 4, i % 4 + 1)
                    q = i // 4
                    if g == "B":
                        link(v.tensor_tensor(expsum[:, m], expsum[:, m], expsink[:, m], ALU.add))
                    link(v.reciprocal(rden[:, m], expsum[:, m]))
                    need(dve, "values_done", l, i + 1)
                    if q >= 2 and h == 0:
                        need(dve, "o_T", l, q - 1)
                    done(v.tensor_scalar_mul(o_attn[:, q % 2, h * HD:(h + 1) * HD], ps[:, 6, 0:HD],
                                        rden[:, m]), "o_read")

                def out_low(q):
                    g, t, _, _ = items[4 * q]
                    need(dve, "o_hi", l, q + 1)
                    ch = 0 if g == "A" else 2
                    c = slice(t * P, (t + 1) * P)
                    done(low(act_lo[:, ch:ch + 2, c], ps[:, 7, 256:512].rearrange("p (k t) -> p k t", t=P),
                        act_hi[:, ch:ch + 2, c]), "o_T_lo")

                need(dve, "pre_ready", l, pre_count(l, 4, len(block_tiles(l, 4)) - 1))
                done(v.memset(mix_bd[:, :, :], 0.0), "mix_zero")
                need(dve, "lg_ln", l, 1)
                v.tensor_scalar_mul(lg[:, 0, :], lg_raw[:, 0:4], -1.0)
                v.tensor_copy(lg[:, 1, :], lg_raw[:, 4:8])
                done(v.tensor_scalar_mul(lg[:, 2, :], lg_raw[:, 4:8], -float(SEQ + P)), "lg_set")
                need(dve, "sink_in", l, 16)
                link(v.tensor_scalar_mul(nsink[:, :], sink[:, :], -1.0))
                for s in range(total + 5):
                    if s < total:
                        maxima(s)
                    if 2 <= s < total + 2:
                        read_T(s - 2)
                    if 3 <= s < total + 3:
                        need(dve, "probs_ready", l, s - 2)
                        output(s - 3)
                    if s >= 4 and (s - 4) % 4 == 3 and s - 4 < total:
                        out_low((s - 4) // 4)
                    if s // 8 < len(fill):
                        mod_terms(fill[s // 8], s % 8)

            def retention(l):
                items = ret_items(l)
                per = len(items) // 4

                def strip_arg(h):
                    link(v.tensor_scalar_mul(strip[:, h % 2, :], delta[:, 0:896], lg[:, 0, h:h + 1]))
                    done(v.scalar_tensor_tensor(strip[:, h % 2, :], delta[:, 0:896], lg[:, 1, h:h + 1], strip[:, h % 2, :],
                                           ALU.mult, ALU.min), "strip_arg")

                def strip_end(h):
                    need(dve, "strip_exp", l, 3 * (h + 1))
                    v.tensor_tensor(strip[:, h % 2, 384:512], strip[:, h % 2, 384:512], ident[:, :], ALU.add)
                    done(v.tensor_tensor(strip_ctx[:, h % 2, :], strip_ctx[:, h % 2, :], ctx_part[:, :], ALU.add), "strip_ready")

                def decays(h):
                    need(dve, "strip_ready", l, h + 1)
                    for i in range(per * h, per * (h + 1)):
                        _, s, lat = items[i]
                        need(dve, "ret_scores", l, i + 1)
                        if i >= 2:
                            need(dve, "ret_values", l, i - 1)
                        n = SEQ if lat else CTX
                        if lat and s < CT:
                            d = strip_ctx[:, h % 2, P - P * s:P - P * s + n]
                        else:
                            k = s - CT if lat else s
                            d = strip[:, h % 2, 384 - P * k:384 - P * k + n]
                        done(v.tensor_tensor(decayed[:, i % 2, 0:n], ps[:, i % 2, 0:n], d, ALU.mult), "decayed_ready")
                        if i // 8 < len(fill):
                            mod_terms(fill[i // 8], i % 8)

                fill = ret_fill(l)
                need(dve, "delta_in", l, 16)
                strip_arg(0)
                strip_end(0)
                strip_arg(1)
                decays(0)
                strip_end(1)
                strip_arg(2)
                decays(1)
                strip_end(2)
                strip_arg(3)
                decays(2)
                strip_end(3)
                decays(3)

            def fourier(l):
                need_ctx = l < DEPTH - 1
                tiles = tiles_of(l)

                def group_norm():
                    for n, t in enumerate(tiles):
                        v.tensor_tensor(gate_ret[:, t, :], gate_ret[:, t, :], gn_w[:, :], ALU.mult)
                        for h in range(4):
                            ins = v.bn_stats(gst[:, n, h, :], o_ret[:, t, h * HD:(h + 1) * HD])
                    link(ins)
                    for n in range(len(tiles)):
                        for h in range(4):
                            ins = v.bn_aggr(gmv[:, n, h, :], gst[:, n, h, :])
                    done(ins, "gvar")
                    need(dve, "gsd", l, 1)
                    link(v.reciprocal(grs[:, 0:len(tiles), :], gsd[:, 0:len(tiles), :]))
                    for n, t in enumerate(tiles):
                        for h in range(4):
                            c = slice(h * HD, (h + 1) * HD)
                            ins = v.tensor_scalar(o_ret[:, t, c], o_ret[:, t, c], gmv[:, n, h, 0:1], grs[:, n, h:h + 1],
                                                  ALU.subtract, ALU.mult)
                        link(ins)
                        done(v.tensor_tensor(o_ret[:, t, :], o_ret[:, t, :], gate_ret[:, t, :], ALU.mult), "y_ret_ready")

                need(dve, "gn_in", l, 16)
                need(dve, "o_ret_ready", l, 4)
                group_norm()
                for n in range(4 if need_ctx else 2):
                    need(dve, "four_hi", l, n + 1)
                    ch = n % 2
                    src, c = (ps[:, 6 + ch, :], slice(CTX, TOK)) if n < 2 else (ps[:, ch, 0:CTX], slice(0, CTX))
                    done(low(act_lo[:, 4 + ch, c], src, act_hi[:, 4 + ch, c]), "four_lo")
                for n, t in enumerate(tiles):
                    need(dve, "y_hi", l, n + 1)
                    c = slice(t * P, (t + 1) * P)
                    done(low(act_lo[:, 6:8, c], ps[:, 4 + n % 2, 0:256].rearrange("p (k t) -> p k t", t=P),
                        act_hi[:, 6:8, c]), "y_lo")

            def up_half(l, fh):
                width, parts = (384, 2) if l < DEPTH - 1 else (512, 1)
                lo_col = 0 if l < DEPTH - 1 else CTX

                def chunk(e, j, ready):
                    need(dve, "silu_ready", l, ready)
                    pat = dict(r=parts)
                    done(v.tensor_tensor(hid[:, j, lo_col:TOK].rearrange("p (r n) -> p r n", **pat),
                                    silu_g[:, e, lo_col:TOK].rearrange("p (r n) -> p r n", **pat),
                                    ps[:, 4 * e + 2:4 * e + 2 + parts, 0:width], ALU.mult), "hid_ready")

                for f in range(HALF):
                    chunk(f % 2, f, fh * HALF + f + 1)
                    if fh == 0 and f >= HALF - 3 and f - (HALF - 3) < 2:
                        for k in range(KC):
                            mod_terms(ffn_fill(l)[f - (HALF - 3)], k)

            def down_low(l, fh):
                tiles = tiles_of(l)
                nt = len(tiles)
                cols = slice(0 if l < DEPTH - 1 else CTX, TOK)

                def lows(p, js):
                    for j in js:
                        hi_, lo_ = hid_slot(p, j)
                        need(dve, "hid_hi", l, p * HALF + j + 1)
                        done(low(lo_[:, cols], hid[:, j, cols], hi_[:, cols]), "hid_split")

                p = 2 * fh
                lows(p, range(HALF))
                lows(p + 1, range(2))
                for n, t in enumerate(tiles):
                    residual(l, "dn", p, n, t, nt, dn_slot(l, p, HALF - 1), 0, fh == 0)
                    if fh == 1:
                        link(half_stats(t, 0, 0))
                lows(p + 1, range(2, HALF))
                if fh == 0:
                    for n, t in enumerate(tiles):
                        residual(l, "dn", p + 1, n, t, nt, dn_slot(l, p + 1, HALF - 1), 1, True)

            link(v.memset(pick[:, :, :], 0.0))
            for o in range(2):
                v.memset(pick[:, o, o:o + 1], 1.0)
            done(v.memset(eps[:, :], EPS), "eps_ready")
            dve.wait_ge(c_ready, 1)
            dve.wait_ge(x_in, 32)
            dve.wait_ge(const_in, 16 * N_CONST)
            norm_steps(("pre", 0), ALL, None)
            for l in range(DEPTH):
                tiles = tiles_of(l)
                nt = len(tiles)
                project(l)
                attention(l)
                retention(l)
                fourier(l)
                dve.wait_ge(mod_out_read, mod_done(l, "modG"))
                last = SLOT0[(l, "wout")] + 7
                for n, t in enumerate(tiles):
                    residual(l, "wout", 0, n, t, nt, last, 0, True)
                    link(half_stats(t, 0, 0))

                def first_1(n, t):
                    residual(l, "wout", 1, n, t, nt, last + 8, 1, True)
                    need(dve, "wout_read", l, nt + n + 1)

                def first_2(n, t):
                    residual(l, "dn", 3, n, t, nt, dn_slot(l, 3, HALF - 1), 1, False)
                    need(dve, "dn_read", l, 3 * nt + n + 1)

                norm_steps((l, 1), tiles, first_1)
                up_half(l, 0)
                dve.wait_ge(mod_out_read, mod_done(l, "modC"))
                down_low(l, 0)
                up_half(l, 1)
                down_low(l, 1)
                norm_steps((l, 2), tiles, first_2)


_INS = ["x", "c", "ctx", "c_ctx", "w_mod", "b_mod", "w_in", "a_q_norm", "a_k_norm", "b_sink", "f_mix", "r_decay",
        "r_gn_w", "w_out", "ln1_w", "ln1_b", "w_gate_up", "w_down", "ln2_w", "ln2_b"]
_OUTS = [((1, SEQ, D), "float32")]


def kernel(**inputs):
    import numpy as _np
    import concourse.bacc as _bacc
    from concourse import mybir as _mybir
    from concourse.bass_utils import run_bass_kernel_spmd as _run

    nc = _bacc.Bacc("TRN2", target_bir_lowering=False, num_devices=1)
    arrays, args = {}, []
    for name in _INS:
        a = _np.ascontiguousarray(inputs[name])
        arrays[f"in_{name}_dram"] = a
        args.append(nc.dram_tensor(f"in_{name}_dram", a.shape, _mybir.dt.from_np(a.dtype), kind="ExternalInput").ap())
    for i, (shape, dtype) in enumerate(_OUTS):
        dt = _mybir.dt.from_np(_np.dtype(dtype))
        args.append(nc.dram_tensor(f"out_{i}_dram", shape, dt, kind="ExternalOutput").ap())
    build(nc, *args)
    r = _run(nc, [arrays], core_ids=[0])
    got = tuple(r.results[0][f"out_{i}_dram"] for i in range(len(_OUTS)))
    return got[0]
```
